# Optimizing a Trainium2 kernel written in Bass

```python
import jax, jax.numpy as jnp
from jax import lax
import numpy as np

D_MODEL = 1024
BATCH = 1
SEQ = 128
DEPTH = 1
DEC_BATCH = 1
DEC_SEQ = 128
PAST_LEN = 128

GRID_W = 64
D_MIX = D_MODEL
CONV_CH = D_MIX // 2
RWKV_DIM = D_MIX - CONV_CH
HEAD_DIM = 64
RWKV_HEADS = RWKV_DIM // HEAD_DIM
CONV_WIDTH = 31
DECAY_LORA = 64
ICLR_LORA = 64
GATE_LORA = 128
N_EXPERTS = 32
TOP_K = 4
D_FF = D_MODEL
SWIGLU_LIMIT = 7.0
SWIGLU_ALPHA = 1.702
ROUTE_BLOCK = 128
RMS_EPS = 1e-6
LN_EPS = 1e-5
GN_EPS = 64e-5
N_MOD = 6
IN_COLS = 2 * CONV_CH + 3 * RWKV_DIM

kernel_name = 'hybrid_conv_rwkv7_moe_diffusion_step'

def rms_norm(x, g):
    xf = x.astype(jnp.float32)
    y = xf * lax.rsqrt(jnp.mean(xf * xf, axis=-1, keepdims=True) + RMS_EPS)
    return (y * g.astype(jnp.float32)).astype(x.dtype)

def layer_norm(x, g, b):
    xf = x.astype(jnp.float32)
    mu = jnp.mean(xf, axis=-1, keepdims=True)
    xc = xf - mu
    var = jnp.mean(xc * xc, axis=-1, keepdims=True)
    return (xc * lax.rsqrt(var + LN_EPS) * g.astype(jnp.float32) + b.astype(jnp.float32)).astype(x.dtype)

def conv_module(glu, conv_w, conv_b, ln_g, ln_b, n_seg):
    b, t, ch = glu.shape
    u = glu.reshape(b * n_seg, t // n_seg, ch)
    u = lax.conv_general_dilated(
        u, conv_w[:, None, :].astype(u.dtype), window_strides=(1,),
        padding=[(CONV_WIDTH // 2, CONV_WIDTH // 2)],
        dimension_numbers=('NWC', 'WIO', 'NWC'), feature_group_count=ch)
    u = (u + conv_b).reshape(b, t, ch)
    return jax.nn.silu(layer_norm(u, ln_g, ln_b))

def wkv_scan(r, decay, a_vec, b_vec, v, k, s0, reverse):
    def step(S, inp):
        r_t, w_t, a_t, b_t, v_t, k_t = inp
        sa = jnp.einsum('bhij,bhj->bhi', S, a_t)
        S = S * w_t[:, :, None, :] + sa[..., None] * b_t[:, :, None, :] + v_t[..., None] * k_t[:, :, None, :]
        return S, jnp.einsum('bhij,bhj->bhi', S, r_t)
    xs = tuple(jnp.moveaxis(z, 1, 0) for z in (r, decay, a_vec, b_vec, v, k))
    s_fin, ys = lax.scan(step, s0.astype(jnp.float32), xs, reverse=reverse)
    return jnp.moveaxis(ys, 0, 1), s_fin

def rwkv_group(h, r, k, v, s0_f, s0_b, p):
    b, t, _ = h.shape
    f32 = jnp.float32
    shp = (b, t, RWKV_HEADS, HEAD_DIM)
    rh = r.astype(f32).reshape(shp)
    kh = k.astype(f32).reshape(shp)
    vh = v.astype(f32).reshape(shp)
    kk = (k * p['rw_k_k']).astype(f32).reshape(shp)
    kk = kk * lax.rsqrt(jnp.maximum(jnp.sum(kk * kk, axis=-1, keepdims=True), 1e-24))
    ka = p['rw_k_a'].astype(f32).reshape(RWKV_HEADS, HEAD_DIM)
    rk = p['rw_r_k'].astype(f32)
    ys, bonus, finals = [], [], []
    for d, (s0, rev) in enumerate(((s0_f, False), (s0_b, True))):
        w_raw = p['rw_w0'][d] + jnp.tanh(h @ p['rw_w1'][d]) @ p['rw_w2'][d]
        w_log = -jax.nn.softplus(-w_raw.astype(f32)) - 0.5
        decay = jnp.exp(-jnp.exp(w_log)).reshape(shp)
        a = jax.nn.sigmoid((p['rw_a0'][d] + (h @ p['rw_a1'][d]) @ p['rw_a2'][d]).astype(f32)).reshape(shp)
        k_d = kh * (1.0 + (a - 1.0) * ka)
        y, s_fin = wkv_scan(rh, decay, -kk, kk * a, vh, k_d, s0, rev)
        ys.append(y)
        bonus.append(jnp.sum(rh * k_d * rk, axis=-1, keepdims=True) * vh)
        finals.append(s_fin)
    o = ys[0] + ys[1]
    mu = jnp.mean(o, axis=-1, keepdims=True)
    oc = o - mu
    o = oc * lax.rsqrt(jnp.mean(oc * oc, axis=-1, keepdims=True) + GN_EPS)
    o = o.reshape(b, t, RWKV_DIM) * p['rw_gn_g'].astype(f32) + p['rw_gn_b'].astype(f32)
    o = o + (bonus[0] + bonus[1]).reshape(b, t, RWKV_DIM)
    g = jax.nn.sigmoid(h @ p['rw_g1']) @ p['rw_g2']
    return (o * g.astype(f32)).astype(h.dtype), finals[0], finals[1]

def routed_ffn(h, p):
    shp = h.shape
    tok = h.reshape(-1, D_MODEL)
    n_tok = tok.shape[0]
    logits = (tok @ p['router_w'] + p['router_b']).astype(jnp.float32)
    top_val, top_idx = lax.top_k(logits, TOP_K)
    gate = jax.nn.softmax(top_val, axis=-1)
    n_assign = n_tok * TOP_K
    flat_e = top_idx.reshape(n_assign).astype(jnp.int32)
    flat_tok = jnp.arange(n_assign, dtype=jnp.int32) // TOP_K
    order = jnp.argsort(flat_e)
    e_sorted = flat_e[order]
    tok_sorted = flat_tok[order]
    gate_sorted = gate.reshape(n_assign)[order]
    counts = jnp.bincount(flat_e, length=N_EXPERTS).astype(jnp.int32)
    padded = (counts + ROUTE_BLOCK - 1) // ROUTE_BLOCK * ROUTE_BLOCK
    pad_end = jnp.cumsum(padded)
    pad_start = pad_end - padded
    start = jnp.cumsum(counts) - counts
    dest = pad_start[e_sorted] + (jnp.arange(n_assign, dtype=jnp.int32) - start[e_sorted])
    n_blocks = -(-n_assign // ROUTE_BLOCK) + N_EXPERTS
    tok_buf = jnp.full((n_blocks * ROUTE_BLOCK,), n_tok, jnp.int32).at[dest].set(tok_sorted)
    gate_buf = jnp.zeros((n_blocks * ROUTE_BLOCK,), jnp.float32).at[dest].set(gate_sorted)
    blk_e = jnp.searchsorted(pad_end, jnp.arange(n_blocks, dtype=jnp.int32) * ROUTE_BLOCK, side='right')
    blk_e = jnp.minimum(blk_e, N_EXPERTS - 1).astype(jnp.int32)
    tok_pad = jnp.concatenate([tok, jnp.zeros((1, D_MODEL), tok.dtype)], axis=0)

    def expert_block(args):
        idx, g, e = args
        xb = tok_pad[idx]
        gu = xb @ p['w_gu'][e] + p['b_gu'][e]
        x_glu, x_lin = gu[:, :D_FF], gu[:, D_FF:]
        x_glu = jnp.minimum(x_glu, SWIGLU_LIMIT)
        x_lin = jnp.clip(x_lin, -SWIGLU_LIMIT, SWIGLU_LIMIT)
        act = x_glu * jax.nn.sigmoid(SWIGLU_ALPHA * x_glu) * (x_lin + 1.0)
        out = act @ p['w_down'][e] + p['b_down'][e]
        return out.astype(jnp.float32) * g[:, None]

    outs = lax.map(expert_block, (tok_buf.reshape(n_blocks, ROUTE_BLOCK),
                                  gate_buf.reshape(n_blocks, ROUTE_BLOCK), blk_e))
    y = jax.ops.segment_sum(outs.reshape(n_blocks * ROUTE_BLOCK, D_MODEL), tok_buf,
                            num_segments=n_tok + 1)[:n_tok]
    return y.astype(h.dtype).reshape(shp)

def trunk_layer(x, mod, s0_f, s0_b, n_seg, p):
    sh1, sc1, gt1, sh2, sc2, gt2 = [mod[:, i][:, None, :] for i in range(N_MOD)]
    h = rms_norm(x, p['pre_mix_g']) * (1.0 + sc1) + sh1
    proj = h @ p['w_in']
    c_val, c_gate, r, k, v = jnp.split(
        proj, [CONV_CH, 2 * CONV_CH, 2 * CONV_CH + RWKV_DIM, 2 * CONV_CH + 2 * RWKV_DIM], axis=-1)
    conv_out = conv_module(c_val * jax.nn.sigmoid(c_gate), p['conv_w'], p['conv_b'],
                           p['conv_ln_g'], p['conv_ln_b'], n_seg)
    rwkv_out, s_f, s_b = rwkv_group(h, r, k, v, s0_f, s0_b, p)
    mix = jnp.concatenate([conv_out, rwkv_out], axis=-1) @ p['w_out']
    x = x + gt1 * rms_norm(mix, p['post_mix_g'])
    h2 = rms_norm(x, p['pre_ffn_g']) * (1.0 + sc2) + sh2
    x = x + gt2 * rms_norm(routed_ffn(h2, p), p['post_ffn_g'])
    return x, s_f, s_b

def _normal(key, shape, scale):
    return scale * jax.random.normal(key, shape, jnp.float32)

def setup_inputs(seed: int = 0) -> dict:
    key = jax.random.key(seed)
    ks = jax.random.split(key, 37)
    L, D = DEPTH, D_MODEL
    st_shape = (DEC_BATCH, DEPTH, RWKV_HEADS, HEAD_DIM, HEAD_DIM)
    return {
        'x_prompt': _normal(ks[0], (BATCH, SEQ, D), 1.0),
        'x_sample': _normal(ks[1], (DEC_BATCH, DEC_SEQ, D), 1.0),
        'state_wkv_fwd': _normal(ks[2], st_shape, 0.3),
        'state_wkv_bwd': _normal(ks[3], st_shape, 0.3),
        'c': _normal(ks[4], (DEC_BATCH, D), 1.0),
        'c_ctx': _normal(ks[5], (D,), 1.0),
        'ada_w': _normal(ks[6], (L, D, N_MOD * D), 0.5 * D ** -0.5),
        'ada_b': _normal(ks[7], (L, N_MOD * D), 0.02),
        'pre_mix_g': 1.0 + _normal(ks[8], (L, D), 0.02),
        'post_mix_g': 1.0 + _normal(ks[9], (L, D), 0.02),
        'pre_ffn_g': 1.0 + _normal(ks[10], (L, D), 0.02),
        'post_ffn_g': 1.0 + _normal(ks[11], (L, D), 0.02),
        'w_in': _normal(ks[12], (L, D, IN_COLS), D ** -0.5),
        'w_out': _normal(ks[13], (L, D_MIX, D), D_MIX ** -0.5),
        'conv_w': _normal(ks[14], (L, CONV_WIDTH, CONV_CH), CONV_WIDTH ** -0.5),
        'conv_b': _normal(ks[15], (L, CONV_CH), 0.02),
        'conv_ln_g': 1.0 + _normal(ks[16], (L, CONV_CH), 0.02),
        'conv_ln_b': _normal(ks[17], (L, CONV_CH), 0.02),
        'rw_w0': 0.5 + _normal(ks[18], (L, 2, RWKV_DIM), 0.5),
        'rw_w1': _normal(ks[19], (L, 2, D, DECAY_LORA), D ** -0.5),
        'rw_w2': _normal(ks[20], (L, 2, DECAY_LORA, RWKV_DIM), 0.5 * DECAY_LORA ** -0.5),
        'rw_a0': _normal(ks[21], (L, 2, RWKV_DIM), 0.3),
        'rw_a1': _normal(ks[22], (L, 2, D, ICLR_LORA), D ** -0.5),
        'rw_a2': _normal(ks[23], (L, 2, ICLR_LORA, RWKV_DIM), 0.5 * ICLR_LORA ** -0.5),
        'rw_g1': _normal(ks[24], (L, D, GATE_LORA), D ** -0.5),
        'rw_g2': _normal(ks[25], (L, GATE_LORA, RWKV_DIM), GATE_LORA ** -0.5),
        'rw_k_k': 0.85 + _normal(ks[26], (L, RWKV_DIM), 0.05),
        'rw_k_a': 1.0 + _normal(ks[27], (L, RWKV_DIM), 0.05),
        'rw_r_k': _normal(ks[28], (L, RWKV_HEADS, HEAD_DIM), 0.1),
        'rw_gn_g': 1.0 + _normal(ks[29], (L, RWKV_DIM), 0.02),
        'rw_gn_b': _normal(ks[30], (L, RWKV_DIM), 0.02),
        'router_w': _normal(ks[31], (L, D, N_EXPERTS), D ** -0.5),
        'router_b': _normal(ks[32], (L, N_EXPERTS), 0.01),
        'w_gu': _normal(ks[33], (L, N_EXPERTS, D, 2 * D_FF), D ** -0.5),
        'b_gu': _normal(ks[34], (L, N_EXPERTS, 2 * D_FF), 0.02),
        'w_down': _normal(ks[35], (L, N_EXPERTS, D_FF, D), D_FF ** -0.5),
        'b_down': _normal(ks[36], (L, N_EXPERTS, D), 0.02),
    }

def reference(x_prompt, x_sample, state_wkv_fwd, state_wkv_bwd, c, c_ctx, ada_w, ada_b,
              pre_mix_g, post_mix_g, pre_ffn_g, post_ffn_g, w_in, w_out, conv_w, conv_b,
              conv_ln_g, conv_ln_b, rw_w0, rw_w1, rw_w2, rw_a0, rw_a1, rw_a2, rw_g1, rw_g2,
              rw_k_k, rw_k_a, rw_r_k, rw_gn_g, rw_gn_b, router_w, router_b, w_gu, b_gu,
              w_down, b_down):
    rows = x_sample.shape[1] // GRID_W
    zero_state = jnp.zeros((x_prompt.shape[0], RWKV_HEADS, HEAD_DIM, HEAD_DIM), jnp.float32)
    y_prompt, y_sample = x_prompt, x_sample
    new_f, new_b = [], []
    for l in range(DEPTH):
        p = {
            'pre_mix_g': pre_mix_g[l], 'post_mix_g': post_mix_g[l],
            'pre_ffn_g': pre_ffn_g[l], 'post_ffn_g': post_ffn_g[l],
            'w_in': w_in[l], 'w_out': w_out[l],
            'conv_w': conv_w[l], 'conv_b': conv_b[l],
            'conv_ln_g': conv_ln_g[l], 'conv_ln_b': conv_ln_b[l],
            'rw_w0': rw_w0[l], 'rw_w1': rw_w1[l], 'rw_w2': rw_w2[l],
            'rw_a0': rw_a0[l], 'rw_a1': rw_a1[l], 'rw_a2': rw_a2[l],
            'rw_g1': rw_g1[l], 'rw_g2': rw_g2[l],
            'rw_k_k': rw_k_k[l], 'rw_k_a': rw_k_a[l], 'rw_r_k': rw_r_k[l],
            'rw_gn_g': rw_gn_g[l], 'rw_gn_b': rw_gn_b[l],
            'router_w': router_w[l], 'router_b': router_b[l],
            'w_gu': w_gu[l], 'b_gu': b_gu[l], 'w_down': w_down[l], 'b_down': b_down[l],
        }
        mod_ctx = (jax.nn.silu(c_ctx) @ ada_w[l] + ada_b[l]).reshape(1, N_MOD, D_MODEL)
        mod_lat = (jax.nn.silu(c) @ ada_w[l] + ada_b[l]).reshape(c.shape[0], N_MOD, D_MODEL)
        y_prompt, s_f, s_b = trunk_layer(y_prompt, mod_ctx, zero_state, zero_state, 1, p)
        new_f.append(s_f)
        new_b.append(s_b)
        y_sample, _, _ = trunk_layer(y_sample, mod_lat, state_wkv_fwd[:, l], state_wkv_bwd[:, l], rows, p)
    new_state_wkv_fwd = jnp.stack(new_f, axis=1)
    new_state_wkv_bwd = jnp.stack(new_b, axis=1)
    return (y_prompt, y_sample, new_state_wkv_fwd, new_state_wkv_bwd)


_drawn_inputs = setup_inputs


def setup_inputs(seed=0):
    import zlib

    import numpy as np

    out = dict(_drawn_inputs(seed))
    spreads = {}
    factors = {'state_wkv_fwd': 8.0,
     'state_wkv_bwd': 6.251,
     'post_mix_g': 4.029,
     'post_ffn_g': 8.0,
     'conv_ln_g': 6.313,
     'conv_ln_b': 7.746,
     'rw_k_k': 4.648,
     'rw_gn_g': 6.216,
     'rw_gn_b': 3.339,
     'b_gu': 8.0,
     'b_down': 8.0}
    for name, (base, spread) in spreads.items():
        noise = np.random.default_rng([zlib.crc32(name.encode()), seed]).standard_normal(out[name].shape)
        drawn = base * np.exp(spread * noise) if base else spread * noise
        out[name] = __import__('jax').numpy.asarray(drawn.astype(out[name].dtype))
    for name, factor in factors.items():
        out[name] = (out[name] * factor).astype(out[name].dtype)
    return out
```

```python
import math
from contextlib import ExitStack

import numpy as np
import concourse.bass as bass
from concourse import mybir

FP32 = mybir.dt.float32
U8 = mybir.dt.uint8
I32 = mybir.dt.int32
ALU = mybir.AluOpType
ACT = mybir.ActivationFunctionType
AX = mybir.AxisListType

P = 128
G = 2
D = 1024
KC = D // P
T = 128
N = G * T
CH = 512
Q = CH // P
HD = 64
TAPS = 31
PAD = TAPS // 2
SEG = 64
LORA = 64
E = 32
TOPK = 4
F = 1024
S = 64
KAPPA = math.exp(-0.5)
LEVELS = 7
U_CTX, U_LAT = PAD, PAD + T + PAD
U_STEP = SEG + PAD
U_COLS = U_LAT + 2 * U_STEP
A_COLS = U_COLS - 2 * PAD
A_LAT = U_LAT - PAD
C_CONVB, C_LNG, C_LNB = TAPS, TAPS + 1, TAPS + 2
C_W0, C_A0 = TAPS + 3, TAPS + 5
C_KK, C_KA, C_RK, C_GNG, C_GNB = (TAPS + 7 + n for n in range(5))
C_N = TAPS + 12
K_ID, K_HEAD, K_ONES, K_UPPER, K_MASK, K_IOTA = 0, 128, 256, 384, 512, 1024
K_EPS = K_IOTA + S
K_ONE = K_EPS + 3
K_N = K_ONE + 3
BIG = 3.0e38
FRONT = 27940


class Steps:

    def __init__(self):
        self.count, self.values = 0, {}

    def mark(self, name):
        self.count += 1
        self.values.setdefault(name, []).append(self.count)
        return 1

    def after(self, name, n):
        return self.values[name][n - 1]


def build(nc, x_in, cond_in, ada_w, mod_in, w_in, w_out, chan_in, lora1_in, w2_in, a2_in, g2_in,
          s0_in, router_w, router_b, w_gu, b_gu, w_down, b_down, const_in, level_in,
          y_prompt, y_sample, st_f, st_b):
    with ExitStack() as ctx:
        def sem(name):
            return ctx.enter_context(nc.semaphore(name))

        ring = ctx.enter_context(nc.sbuf_tensor("ring", [P, 24576], FP32))
        front = ctx.enter_context(nc.sbuf_tensor("front", [P, FRONT], FP32))
        level = ctx.enter_context(nc.sbuf_tensor("level", [P, LEVELS, 3, T], U8))
        ps = [ctx.enter_context(nc.psum_tensor(f"bank{n}", [P, 512], FP32))[:, :] for n in range(8)]
        top = [0]

        def take(words):
            top[0] += words
            assert top[0] <= FRONT, top[0]
            return front[:, top[0] - words:top[0]]

        def view(ap, pattern, **sizes):
            return ap.rearrange(pattern, **sizes)

        const = take(K_N)
        chan = view(take(Q * C_N), "p (q c) -> p q c", q=Q)
        r_hT, r_V, r_rk, r_kk = take(2048), take(1024), take(2048), take(1024)
        r_r, r_k = r_rk[:, 0:1024], r_rk[:, 1024:2048]
        r_a, r_P = take(2048), take(2 * Q * G * (T + 1))
        r_o, r_u = take(1024), take(Q * U_COLS)
        r_L = take(5240)
        g2 = take(512)
        r_mid = take(768)
        r_ra, r_E, r_kb, r_S0 = take(2048), take(1032), take(1024), take(512)
        r_mod = take(1024)
        siluT = view(take(KC * 32), "p (k m) -> p k m", k=KC)
        r_bk, r_S = take(512), take(512)
        small = take(240)

        ident = const[:, K_ID:K_ID + P]
        head_ones = const[:, K_HEAD:K_HEAD + P]
        ones = const[:, K_ONES:K_ONES + P]
        upper = const[:, K_UPPER:K_UPPER + P]
        mask_lt = view(const[:, K_MASK:K_MASK + 512], "p (d a t) -> p d a t", d=2, a=2)
        iota = const[:, K_IOTA:K_IOTA + S]
        eps = [const[:, K_EPS + n:K_EPS + n + 1] for n in range(3)]

        ada0 = view(ring[:, 0:16384], "p (k n) -> p k n", k=KC)
        x0 = view(r_P[:, 0:2048], "p (g d) -> p g d", g=G)
        xn = view(r_a, "p (g d) -> p g d", g=G)
        modT = view(r_kb[:, 0:512], "p (m r) -> p m r", m=4)
        mod0 = r_E[:, 0:512]
        madd0, mmul0 = r_ra[:, 0:512], r_ra[:, 512:1024]
        madd, mmul = (view(r_hT[:, 1024 * n:1024 * (n + 1)], "p (b n) -> p b n", b=2) for n in range(2))
        mod = view(r_mod, "p (b n) -> p b n", b=2)
        hT = view(r_hT, "p (c t) -> p c t", c=KC)
        level_f = view(r_rk[:, 0:LEVELS * 2 * T], "p (n a t) -> p n a t", n=LEVELS, a=2)
        win_at = [16384 + 2560 * k if k < 3 else 2560 * (k - 3) for k in range(KC)]
        win = [ring[:, a:a + 2560] for a in win_at]
        lora1 = view(r_L[:, 0:3072], "p (k r) -> p k r", k=KC)
        w2p = view(r_L[:, 3072:4096], "p (d n) -> p d n", d=2)
        a2p = view(r_L[:, 4096:5120], "p (d n) -> p d n", d=2)
        mids = view(r_mid, "p (a t) -> p a t", a=3)
        sgw = view(r_ra, "p (n t) -> p n t", n=8)
        V = view(r_V, "p (g n) -> p g n", g=G)
        rT, kT, kkT = (view(a, "p (q t) -> p q t", q=Q) for a in (r_r, r_k, r_kk))
        aT = view(r_a, "p (d q t) -> p d q t", d=2, q=Q)
        Pc = view(r_P, "p (d q g t) -> p d q g t", d=2, q=Q, g=G)
        sgc = view(r_o, "p (q t) -> p q t", q=Q)
        u = view(r_u, "p (q t) -> p q t", q=Q)
        kbp = view(r_L[:, 0:2048], "p (g k h d t) -> p g k h d t", g=G, k=2, h=2, d=2)
        dgm = view(r_L[:, 2048:2560], "p (w d j) -> p w d j", w=2, d=2)
        S0s = view(r_L[:, 2560:3072], "p (w d j) -> p w d j", w=2, d=2)
        acc = view(r_L[:, 3072:3072 + Q * A_COLS], "p (q t) -> p q t", q=Q)
        rkk = view(r_L[:, 4216:5240], "p (q t) -> p q t", q=Q)
        sqk, rn = rkk, view(r_ra[:, 0:1024], "p (q t) -> p q t", q=Q)
        ra = view(r_ra, "p (w g d k t) -> p w g d k t", w=2, g=G, d=2, k=2)
        Ex = view(r_E, "p (s d g t) -> p s d g t", s=2, d=2, g=G)
        kd = view(r_kb[:, 0:512], "p (d t) -> p d t", d=2)
        bv = view(r_kb[:, 512:1024], "p (d t) -> p d t", d=2)
        S0 = view(r_S0, "p (w d j) -> p w d j", w=2, d=2)
        bkT = view(r_bk, "p (k d j) -> p k d j", k=2, d=2)
        stS = view(r_S, "p (d q j) -> p d q j", d=2, q=Q)
        oT = view(r_o, "p (q t) -> p q t", q=Q)
        LT = view(ring[:, 16384:20480], "p (g h d k t) -> p g h d k t", g=G, h=2, d=2, k=4)
        X, Y, Pn = (view(ring[:, 20480 + 1024 * n:21504 + 1024 * n], "p (g h d t) -> p g h d t", g=G, h=2, d=2)
                    for n in range(3))
        W, SA = (view(ring[:, 23552 + 512 * n:24064 + 512 * n], "p (g d i) -> p g d i", g=G, d=2)
                 for n in range(2))
        ada_slot = view(ring[:, 0:8192], "p (k n) -> p k n", k=4)
        wout = view(ring[:, 8192:16384], "p (k n) -> p k n", k=KC)
        oc = view(ring[:, 16384:17408], "p (q t) -> p q t", q=Q)
        sq = view(ring[:, 17408:18432], "p (q t) -> p q t", q=Q)
        vT, gT = kT, rT
        csq = view(r_u[:, 0:Q * A_COLS], "p (q t) -> p q t", q=Q)
        cvT = view(ring[:, 18432:19456], "p (q t) -> p q t", q=Q)
        crs = ring[:, 19456:19456 + A_COLS]
        csg = view(ring[:, 20480:20480 + Q * A_COLS], "p (q t) -> p q t", q=Q)
        mixn = view(r_a, "p (g d) -> p g d", g=G)
        x1 = view(r_P[:, 0:2048], "p (g d) -> p g d", g=G)
        h2 = view(r_L[:, 0:2048], "p (g d) -> p g d", g=G)
        h2T = hT
        rw = view(r_S0[:, 0:256], "p (k e) -> p k e", k=KC)
        rb = r_S0[:, 256:256 + E]
        wgu = view(ring[:, 0:16384], "p (k n) -> p k n", k=KC)
        wdn = view(ring[:, 16384:24576], "p (k n) -> p k n", k=KC)
        bgu = r_ra[0:E, :]
        bdn = r_kb[0:E, :]
        sel = view(r_E[:, 0:256], "p (g q s) -> p g q s", g=G, q=2)
        selg = view(r_E[:, 256:512], "p (g q s) -> p g q s", g=G, q=2)
        bsel = view(r_E[0:E, 512:640], "p (q s) -> p q s", q=2)
        GT = view(r_E[:, 640:896], "p (g t) -> p g t", g=G)
        xT = view(r_V, "p (c s) -> p c s", c=KC)
        glu, lin = r_r[:, 0:512], r_r[:, 512:1024]
        sig, act = r_k[:, 0:512], r_k[:, 512:1024]
        actT = view(r_kk[:, 0:512], "p (m s) -> p m s", m=4)
        outp = r_o
        yacc = view(r_a, "p (g d) -> p g d", g=G)
        junk0, junk = r_o, r_u[:, 0:1024]
        at = [0]

        def tiny(n):
            at[0] += n
            assert at[0] <= 240
            return small[:, at[0] - n:at[0]]

        ssx, rsx, ssm, rsm, ss2, rs2 = (tiny(4) for _ in range(6))
        omka = tiny(Q)
        ext = view(tiny(G * 40), "p (g e) -> p g e", g=G)
        m8 = view(r_bk[:, 0:16], "p (g e) -> p g e", g=G)
        b8 = view(r_bk[:, 16:32], "p (g e) -> p g e", g=G)
        rep = view(r_bk[:, 32:112], "p (g e) -> p g e", g=G)
        sel_m = view(r_bk[:, 112:176], "p (g e) -> p g e", g=G)
        ex = view(r_bk[:, 176:240], "p (g e) -> p g e", g=G)
        gsum = r_bk[:, 240:242]
        grec = r_bk[:, 242:244]
        negm = r_bk[:, 244:246]
        most = r_bk[:, 246:247]
        gate = view(tiny(G * E), "p (g e) -> p g e", g=G)
        rank = view(tiny(G * E), "p (g e) -> p g e", g=G)
        most_i = tiny(1).bitcast(I32)
        gateT = r_bk[0:E, 256:512]

        names = """in_win level in_x in_const in_cond in_mod in_lora in_rw in_wout in_x1 in_router st_out y_out silu_pad
            silu_sig silu rs_x xn xT_tr ada0_acc mod0 mod0_tr modT hT_a hT_v l2_mm pre scan a_sig pool_zero
            kv_mm kk_raw kk_sq kk_mm kk_sqrt kk ex kdb prep_s prep s0_in rsum m_mm m_ev bt_mm bt_ev xy d_mm
            x_up y_up p_mm p_ev e_mm w_mm w_ev sa_mm sa_ev y_mm o_ev st_mm st_ev ada_acc mod_t mod conv
            cm_mm c_cen c_sq cv_mm c_std c_n2 c_sig c_out vt_mm vt gt gt_mm bo_mm bo gn_mm gn_cen gn_sq
            gv_mm gn_std gn_out mix_mm mix_ss mix_rs mix_rec mixn gtb mul1 x1 rs_2 a2b b2b h2 h2T_tr h2T
            logits selm negm expm gate rk_mm rank2 flag gT_tr gT_ev yi_mm yi sel_ready gathered xt_ready
            gu_used glu_ready lin_ready sig_done act_tmp act_ready act_tr actT_ready dn_used outp_ready
            gt_tr gt_ready combined y_added shifted y_rs gt2 fin v_step a_step po_step""".split()
        assert len(set(names)) == len(names)
        s = {n: sem(n) for n in names}
        in_ada = [sem(f"in_ada_{k}") for k in range(4)]
        in_gu = [sem(f"in_wide_{k}") for k in range(KC)]
        in_ada0 = in_gu
        in_dn = [sem(f"in_dn_{k}") for k in range(KC)]

        from_block = ctx.enter_context(nc.Block())
        block = from_block

        items = [("l1", n, 0, "a") for n in range(3)]
        items += [("w", q, d, "a") for q in range(Q) for d in range(2)]
        items += [("a", q, d, "a") for q in range(Q) for d in range(2)]
        items += [("k", q, 0, "a") for q in range(Q)]
        items += [("r", q, 0, "v") for q in range(Q)]
        items += [("kn", q, 0, "v") for q in range(Q)]
        items += [("v", g, 0, "v") for g in range(G)]
        items += [x for q in range(Q) for x in (("cg", q, 0, "a"), ("cv", q, 0, "v"))]
        FIRST = 5

        def emptied(n, engine):
            return sum(1 for it in items[:n] if it[3] == engine)

        def bank_of(n):
            return ps[(FIRST + n) % 8]

        def gu_src(e, k):
            return w_gu[bass.ds(e, 1), k * P:(k + 1) * P, :].rearrange("e p n -> p (e n)")

        def dn_src(e, k):
            return w_down[bass.ds(e, 1), k * P:(k + 1) * P, :].rearrange("e p n -> p (e n)")

        @block.sync
        def _(sp):
            sp.dma_start(x0, x_in.rearrange("(g p) d -> p g d", p=P)).then_inc(s["in_x"], 16)
            for k in range(KC):
                sp.dma_start(ada0[:, k, :], ada_w[k * P:(k + 1) * P, 0:2048]).then_inc(in_ada0[k], 16)
            sp.dma_start(lora1, lora1_in).then_inc(s["in_lora"], 16)
            for d in range(2):
                if d == 0:
                    sp.wait_ge(s["pool_zero"], 1)
                sp.dma_start(w2p[64 * d:64 * d + 64, d, :], w2_in[d]).then_inc(s["in_lora"], 16)
                sp.dma_start(a2p[64 * d:64 * d + 64, d, :], a2_in[d]).then_inc(s["in_lora"], 16)
            sp.dma_start(g2, g2_in).then_inc(s["in_lora"], 16)
            for k in range(KC):
                if k == 3:
                    sp.wait_ge(s["ada0_acc"], KC)
                sp.dma_start(win[k], w_in[k * P:(k + 1) * P, :]).then_inc(s["in_win"], 16)
            sp.wait_ge(s["kv_mm"], len(items) - 3 - 16)
            sp.dma_start(madd, mod_in[0, :, 512:1536].rearrange("p (b n) -> p b n", b=2)).then_inc(s["in_mod"], 16)
            sp.dma_start(mmul, mod_in[1, :, 512:1536].rearrange("p (b n) -> p b n", b=2)).then_inc(s["in_mod"], 16)
            for c in range(16):
                b, k = divmod(c, KC)
                if c >= 4:
                    sp.wait_ge(s["ada_acc"], c - 3)
                if c == 4:
                    sp.dma_start(wout, w_out.rearrange("(k p) n -> p k n", p=P)).then_inc(s["in_wout"], 16)
                sp.dma_start(ada_slot[:, c % 4, :], ada_w[k * P:(k + 1) * P, 2048 * (b + 1):2048 * (b + 2)])\
                    .then_inc(in_ada[c % 4], 16)
            sp.wait_ge(s["st_ev"], 2 * Q)
            for d, out in enumerate((st_f, st_b)):
                sp.dma_start(out.rearrange("(q h) i j -> (h i) q j", h=2), stS[:, d]).then_inc(s["st_out"], 16)
            sp.wait_ge(s["ex"], Q)
            sp.dma_start(x1, x_in.rearrange("(g p) d -> p g d", p=P)).then_inc(s["in_x1"], 16)
            sp.wait_ge(s["prep"], Q)
            sp.wait_ge(s["ada_acc"], 16)
            for k in range(4):
                sp.dma_start(wgu[:, k, :], gu_src(0, k)).then_inc(in_gu[k], 16)
            sp.wait_ge(s["mix_mm"], 2 * G)
            for k in range(4, KC):
                sp.dma_start(wgu[:, k, :], gu_src(0, k)).then_inc(in_gu[k], 16)
            for k in range(KC):
                sp.dma_start(wdn[:, k, :], dn_src(0, k)).then_inc(in_dn[k], 16)

            def load_next(base, e):
                for k in range(KC):
                    sp.wait_ge(s["gu_used"], (base + e) * KC + (k + 1))
                    sp.dma_start(wgu[:, k, :], gu_src(e + 1, k)).then_inc(in_gu[k], 16)
                for k in range(KC):
                    sp.wait_ge(s["dn_used"], (base + e) * KC + (k + 1))
                    sp.dma_start(wdn[:, k, :], dn_src(e + 1, k)).then_inc(in_dn[k], 16)

            with sp.Fori(0, E - 1) as e:
                load_next(0, e)
            sp.wait_ge(s["flag"], 1)
            more = sp.value_load(most_i[0:1, 0:1], min_val=0, max_val=N)
            with sp.If(more > S):
                with sp.Fori(1, N // S) as turn:
                    for k in range(KC):
                        sp.wait_ge(s["gu_used"], turn * (E * KC))
                        sp.dma_start(wgu[:, k, :], gu_src(0, k)).then_inc(in_gu[k], 16)
                    for k in range(KC):
                        sp.wait_ge(s["dn_used"], turn * (E * KC))
                        sp.dma_start(wdn[:, k, :], dn_src(0, k)).then_inc(in_dn[k], 16)
                    with sp.Fori(0, E - 1) as e:
                        load_next(turn * E, e)
            for g, out in enumerate((y_prompt, y_sample)):
                sp.wait_ge(s["fin"], 2 * (g + 1))
                sp.dma_start(out, x1[:, g, :]).then_inc(s["y_out"], 16)
            sp.wait_ge(s["st_out"], 32)
            sp.wait_ge(s["y_out"], 32)

        def pe_pair(pe, base, i):
            n = base + i
            pe.wait_ge(s["sel_ready"], n + 1)
            for c in range(KC):
                for g in range(G):
                    last = pe.matmul(ps[4 + c // 4][:, (c % 4) * P:(c % 4 + 1) * P], h2[:, g, c * P:(c + 1) * P],
                                     sel[:, g].rearrange("p q s -> p (q s)"), start=(g == 0), stop=(g == G - 1))
                if c % 4 == 3:
                    last.then_inc(s["gathered"], 1)
            for q in range(2):
                arrived = pe.snap(n * 32 + 16 * (q + 1))
                if q == 0:
                    pe.wait_ge(s["xt_ready"], n * 2 + 2)
                for r in range(2):
                    for hf in range(2):
                        pe.matmul(ps[r][64 * hf:64 * hf + 64, :], bsel[:, q, :],
                                  bgu[:, r * F + hf * 512:r * F + hf * 512 + 512], start=True, stop=False)
                for k in range(KC):
                    pe.wait_ge(in_gu[k], arrived + 16)
                    for r in range(2):
                        for hf in range(2):
                            last = pe.matmul(ps[r][64 * hf:64 * hf + 64, :], xT[:, k, S * q:S * q + S],
                                             wgu[:, k, r * F + hf * 512:r * F + hf * 512 + 512],
                                             start=False, stop=(k == KC - 1))
                    last.then_inc(s["gu_used"], 1)
                if q == 1:
                    for g in range(G):
                        last = pe.transpose(ps[6][:, g * P:(g + 1) * P], selg[:, g].rearrange("p q s -> p (q s)"), ident)
                    last.then_inc(s["gt_tr"], 1)
                pe.wait_ge(s["act_ready"], n * 2 + (q + 1))
                for m in range(4):
                    last = pe.transpose(ps[3][:, m * P:(m + 1) * P], act[:, m * P:(m + 1) * P], ident)
                last.then_inc(s["act_tr"], 1)
                pe.wait_ge(s["actT_ready"], n * 2 + (q + 1))
                if q == 1:
                    pe.wait_ge(s["outp_ready"], n * 4 + 2)
                for k in range(KC):
                    pe.wait_ge(in_dn[k], arrived)
                    hf, m = divmod(k, 4)
                    for c in range(2):
                        last = pe.matmul(ps[2][64 * c:64 * c + 64, :], actT[:, m, 64 * hf:64 * hf + 64],
                                         wdn[:, k, c * 512:(c + 1) * 512], start=(k == 0), stop=(k == KC - 1))
                    last.then_inc(s["dn_used"], 1)
            pe.wait_ge(s["gt_ready"], n + 1)
            pe.wait_ge(s["outp_ready"], n * 4 + 4)
            for g in range(G):
                for c in range(2):
                    pe.matmul(ps[4 + 2 * g + c], GT[:, g, :], outp[:, c * 512:(c + 1) * 512],
                              start=True, stop=True).then_inc(s["combined"], 1)

        @block.tensor
        def _(pe):
            pe.wait_ge(s["in_const"], 32)
            pe.wait_ge(s["xn"], 2)
            for c in range(KC):
                for g in range(G):
                    last = pe.transpose(ps[1 + 2 * g + c // 4][:, (c % 4) * T:(c % 4 + 1) * T],
                                        xn[:, g, c * P:(c + 1) * P], ident)
                last.then_inc(s["xT_tr"], 1)
            pe.wait_ge(s["silu"], 1)
            for k in range(KC):
                pe.wait_ge(in_ada0[k], 16)
                for j in range(4):
                    last = pe.matmul(ps[0][32 * j:32 * j + 32, :], siluT[:, k, :], ada0[:, k, j * 512:(j + 1) * 512],
                                     start=(k == 0), stop=(k == KC - 1))
                last.then_inc(s["ada0_acc"], 1)
            pe.wait_ge(s["mod0"], 1)
            for m in range(4):
                last = pe.transpose(ps[5][:, m * P:(m + 1) * P], mod0[:, m * P:(m + 1) * P], ident)
            last.then_inc(s["mod0_tr"], 1)
            for n, (kind, q, d, _e) in enumerate(items):
                out = bank_of(n)
                if n == 0:
                    pe.wait_ge(s["in_lora"], 96)
                    pe.wait_ge(s["hT_a"], KC)
                    pe.wait_ge(s["hT_v"], KC)
                    pe.wait_ge(s["modT"], 1)
                if n >= 8:
                    if items[n - 8][3] == "a":
                        pe.wait_ge(s["a_sig"], emptied(n - 7, "a"))
                    else:
                        pe.wait_ge(s["kk"], emptied(n - 7, "v"))
                if kind == "l1":
                    for k in range(KC):
                        last = pe.matmul(out[:, 0:N], lora1[:, k, q * P:(q + 1) * P], hT[:, k, :],
                                         start=(k == 0), stop=(k == KC - 1))
                elif kind in "wa":
                    pe.wait_ge(s["a_sig"], 3)
                    w2 = w2p if kind == "w" else a2p
                    last = pe.matmul(out[:, 0:N], w2[:, d, q * P:(q + 1) * P], mids[:, "wa".index(kind), :],
                                     start=True, stop=True)
                elif kind == "kn":
                    pe.wait_ge(s["kk_sq"], q + 1)
                    last = pe.matmul(out[:, 0:N], head_ones, sqk[:, q, :], start=True, stop=True)
                elif kind == "v":
                    for k in range(KC):
                        last = pe.matmul(out, hT[:, k, q * T:(q + 1) * T], win[k][:, 2 * CH + 2 * CH:2 * CH + 3 * CH],
                                         start=(k == 0), stop=(k == KC - 1))
                else:
                    col = {"cv": 0, "cg": CH, "r": 2 * CH, "k": 3 * CH}[kind] + q * P
                    for k in range(KC):
                        if kind == "k" and q == 0 and k == 0:
                            pe.wait_ge(s["in_win"], 16 * KC)
                        last = pe.matmul(out[:, 0:N], win[k][:, col:col + P], hT[:, k, :],
                                         start=(k == 0), stop=(k == KC - 1))
                last.then_inc(s["kv_mm"] if n >= 19 else s["l2_mm"], 1)

            def ada_part(part):
                b, k0 = part // 2, 4 * (part % 2)
                for k in range(4):
                    pe.wait_ge(in_ada[k], 16 * (part + 1))
                    for j in range(4):
                        last = pe.matmul(ps[6][32 * j:32 * j + 32, :], siluT[:, k0 + k, :],
                                         ada_slot[:, k, j * 512:(j + 1) * 512], start=(k == 0), stop=(k == 3))
                    last.then_inc(s["ada_acc"], 1)

            for q in range(Q):
                w = q % 2
                pe.wait_ge(s["prep"], q + 1)
                pe.wait_ge(s["prep_s"], q + 1)
                if q == 0:
                    pe.wait_ge(s["a_sig"], emptied(len(items), "a"))
                    pe.wait_ge(s["kk"], emptied(len(items), "v"))
                for g in range(G):
                    for i in range(4):
                        h, d = divmod(i, 2)
                        n = 8 * q + 4 * g + i
                        if n >= 2:
                            pe.wait_ge(s["m_ev"], n - 1)
                        if i < 2 and g == 0 and q > 0:
                            pe.wait_ge(s["sa_ev"], 2 * q)
                            pe.wait_ge(s["mod_t"], q)
                        for k in range(2):
                            last = pe.matmul(ps[6 + n % 2][:, 256 * k:256 * k + 256], kbp[:, g, k, h, d, :],
                                             ra[:, w, g, d].rearrange("p k t -> p (k t)"), start=True, stop=True)
                        last.then_inc(s["m_mm"], 1)
                if q > 0:
                    pe.wait_ge(s["x_up"], 12 * q)
                for k in range(2):
                    for d in range(2):
                        for h in range(2):
                            last = pe.matmul(ps[4][:, (2 * k + d) * P:(2 * k + d + 1) * P], kbp[:, 0, k, h, d, :],
                                             dgm[:, w, d, :], start=(h == 0), stop=(h == 1))
                last.then_inc(s["bt_mm"], 1)
                pe.wait_ge(s["m_ev"], 8 * q + 8)
                for g in range(G):
                    if g == 0 and q > 0:
                        pe.wait_ge(s["st_ev"], 2 * q)
                    if g == 1:
                        pe.wait_ge(s["bt_ev"], q + 1)
                    for i in range(4):
                        h, d = divmod(i, 2)
                        last = pe.matmul(ps[2 + 2 * g][:, i * P:(i + 1) * P], LT[:, g, h, d, 3, :], ident,
                                         start=True, stop=True)
                    last.then_inc(s["d_mm"], 1)
                for g in range(G):
                    if g == 1:
                        for d in range(2):
                            pe.matmul(ps[7][:, d * P:(d + 1) * P], ra[:, w, 1, d, 1, :], S0s[:, w, d, :],
                                      start=(d == 0), stop=False, skip_group_check=True)
                    for i in range(4):
                        h, d = divmod(i, 2)
                        last = pe.matmul(ps[6 + g][:, d * P + h * HD:d * P + h * HD + HD], LT[:, g, h, d, 1, :],
                                         V[:, g, q * P + h * HD:q * P + h * HD + HD],
                                         start=(g == 0), stop=True, skip_group_check=True)
                    last.then_inc(s["w_mm"], 1)
                for lv in range(1, LEVELS):
                    for g in range(G):
                        pe.wait_ge(s["x_up"], 12 * q + 2 * (lv - 1) + g + 1)
                        if lv == 1 and q > 0:
                            pe.wait_ge(s["o_ev"], 2 * (q - 1) + g + 1)
                        for i in range(4):
                            h, d = divmod(i, 2)
                            last = pe.matmul(ps[g][:, i * P:(i + 1) * P], LT[:, g, h, d, 3, :], X[:, g, h, d, :],
                                             start=True, stop=True)
                        last.then_inc(s["p_mm"], 1)
                    for g in range(G):
                        pe.wait_ge(s["p_ev"], 12 * q + 2 * (lv - 1) + g + 1)
                        pe.wait_ge(s["y_up"], 14 * q + 2 * (lv - 1) + g + 1)
                        if lv < LEVELS - 1:
                            for i in range(4):
                                h, d = divmod(i, 2)
                                last = pe.matmul(ps[2 + 2 * g][:, i * P:(i + 1) * P], Y[:, g, h, d, :],
                                                 Pn[:, g, h, d, :], start=True, stop=True)
                            last.then_inc(s["d_mm"], 1)
                        for i in range(4):
                            h, d = divmod(i, 2)
                            last = pe.matmul(ps[3 + 2 * g][:, i * P:(i + 1) * P], Pn[:, g, h, d, :],
                                             Y[:, g, h, d, :], start=True, stop=True)
                        last.then_inc(s["e_mm"], 1)
                for g in range(G):
                    pe.wait_ge(s["y_up"], 14 * q + 12 + g + 1)
                    pe.wait_ge(s["w_ev"], 2 * q + g + 1)
                    for i in range(4):
                        h, d = divmod(i, 2)
                        c = d * P + h * HD
                        last = pe.matmul(ps[6 + g][:, 256 + c:256 + c + HD], Y[:, g, h, d, :],
                                         W[:, g, d, h * HD:h * HD + HD], start=True, stop=True)
                    last.then_inc(s["sa_mm"], 1)
                for g in range(G):
                    if g == 1:
                        for d in range(2):
                            pe.matmul(ps[1][:, 0:T], S0s[:, w, d, :], ra[:, w, 1, d, 0, :], start=(d == 0),
                                      stop=False, skip_group_check=True)
                    for i in range(4):
                        h, d = divmod(i, 2)
                        pe.matmul(ps[g][HD * h:HD * h + HD, 0:T], V[:, g, q * P + h * HD:q * P + h * HD + HD],
                                  LT[:, g, h, d, 0, :], start=(g == 0 and d == 0), stop=False, skip_group_check=True)
                    pe.wait_ge(s["sa_ev"], 2 * q + g + 1)
                    for i in range(4):
                        h, d = divmod(i, 2)
                        last = pe.matmul(ps[g][HD * h:HD * h + HD, 0:T], SA[:, g, d, h * HD:h * HD + HD],
                                         LT[:, g, h, d, 2, :], start=False, stop=(d == 1), skip_group_check=True)
                    last.then_inc(s["y_mm"], 1)
                for d in range(2):
                    pe.matmul(ps[2][:, d * P:(d + 1) * P], SA[:, 0, d, :], bkT[:, 1, d, :], start=True, stop=False)
                    last = pe.matmul(ps[2][:, d * P:(d + 1) * P], V[:, 0, q * P:(q + 1) * P], bkT[:, 0, d, :],
                                     start=False, stop=True)
                last.then_inc(s["st_mm"], 1)
                ada_part(q)

            pe.wait_ge(s["rsum"], 3 * Q)
            for g in range(G):
                for q in range(Q):
                    last = pe.transpose(ps[4][:, q * P:(q + 1) * P] if g == 0 else ps[5][:, q * P:(q + 1) * P],
                                        V[:, g, q * P:(q + 1) * P], ident)
                last.then_inc(s["vt_mm"], 1)
            pe.wait_ge(s["o_ev"], 2 * Q)
            for q in range(Q):
                last = pe.matmul(ps[q // 2][:, (q % 2) * N:(q % 2 + 1) * N], head_ones, oT[:, q, :], start=True, stop=True)
                if q % 2:
                    last.then_inc(s["gn_mm"], 1)
            pe.wait_ge(s["sa_ev"], 2 * Q)
            pe.wait_ge(s["st_ev"], 2 * Q)
            for q in range(Q):
                last = pe.matmul(ps[(2, 7)[q // 2]][:, (q % 2) * N:(q % 2 + 1) * N], head_ones, rkk[:, q, :],
                                 start=True, stop=True)
                if q % 2:
                    last.then_inc(s["bo_mm"], 1)
            pe.wait_ge(s["conv"], TAPS * Q)
            for q in range(Q):
                last = pe.matmul(ps[3][:, 0:A_COLS], ones, acc[:, q, :], start=(q == 0), stop=(q == Q - 1))
            last.then_inc(s["cm_mm"], 1)
            pe.wait_ge(s["vt"], 2)
            for q in range(Q):
                last = pe.matmul(ps[4 + q // 2][:, (q % 2) * N:(q % 2 + 1) * N], g2[:, q * P:(q + 1) * P], mids[:, 2, :],
                                 start=True, stop=True)
                if q % 2:
                    last.then_inc(s["gt_mm"], 1)
            pe.wait_ge(s["gn_sq"], 2)
            for q in range(Q):
                last = pe.matmul(ps[q // 2][:, (q % 2) * N:(q % 2 + 1) * N], head_ones, sq[:, q, :], start=True, stop=True)
                if q % 2:
                    last.then_inc(s["gv_mm"], 1)
            pe.wait_ge(s["c_sq"], 1)
            for q in range(Q):
                last = pe.matmul(ps[3][:, 0:A_COLS], ones, csq[:, q, :], start=(q == 0), stop=(q == Q - 1))
            last.then_inc(s["cv_mm"], 1)
            pe.wait_ge(s["in_wout"], 16)
            pe.wait_ge(s["c_out"], Q)
            pe.wait_ge(s["gn_out"], 2)
            for g in range(G):
                for c in range(2):
                    for k in range(KC):
                        lhs = cvT[:, k, g * T:(g + 1) * T] if k < Q else oT[:, k - Q, g * T:(g + 1) * T]
                        last = pe.matmul(ps[2 * g + c], lhs, wout[:, k, c * 512:(c + 1) * 512],
                                         start=(k == 0), stop=(k == KC - 1))
                    last.then_inc(s["mix_mm"], 1)

            def spread(b, j0, banks):
                for g in range(G):
                    for c in range(2):
                        row = 32 * (j0 + c) + g
                        last = pe.matmul(ps[banks + 2 * g + c], ident[:, row:row + 1].broadcast_to([P, P]), mod[:, b, :],
                                         start=True, stop=True)
                return last

            pe.wait_ge(s["mod"], 2)
            pe.wait_ge(s["bo"], 2)
            pe.wait_ge(s["gt"], 2)
            spread(0, 0, 4).then_inc(s["gtb"], 1)
            pe.wait_ge(s["mixn"], 4)
            spread(1, 0, 0).then_inc(s["a2b"], 1)
            pe.wait_ge(s["mul1"], 4)
            spread(0, 2, 4).then_inc(s["b2b"], 1)
            for g in range(G):
                pe.wait_ge(s["h2"], 2 * g + 2)
                for c in range(KC):
                    last = pe.transpose(ps[2 * g + c // 4][:, (c % 4) * P:(c % 4 + 1) * P], h2[:, g, c * P:(c + 1) * P], ident)
                    if c % 4 == 3:
                        last.then_inc(s["h2T_tr"], 1)
            pe.wait_ge(s["in_router"], 16 * 4)
            for g in range(G):
                pe.wait_ge(s["h2T"], 2 * g + 2)
                for c in range(KC):
                    last = pe.matmul(ps[4][:, g * E:(g + 1) * E], h2T[:, c, g * T:(g + 1) * T], rw[:, c, :],
                                     start=(c == 0), stop=(c == KC - 1))
            last.then_inc(s["logits"], 1)
            pe.wait_ge(s["selm"], 2)
            pe.matmul(ps[5][:, 0:E], upper, sel_m[:, 0, :], start=True, stop=True)
            pe.matmul(ps[5][:, E:2 * E], upper, sel_m[:, 1, :], start=True, stop=False)
            pe.matmul(ps[5][:, E:2 * E], ones, sel_m[:, 0, :], start=False, stop=True)
            for g in range(G):
                last = pe.matmul(ps[5][:, 2 * E:3 * E], ones, sel_m[:, g, :], start=(g == 0), stop=(g == 1))
            last.then_inc(s["rk_mm"], 1)
            pe.wait_ge(s["gate"], 2)
            for g in range(G):
                last = pe.transpose(ps[6][0:E, g * T:(g + 1) * T], gate[:, g, :], ident)
            last.then_inc(s["gT_tr"], 1)
            pe.wait_ge(s["gT_ev"], 1)
            for g in range(G):
                for c in range(2):
                    last = pe.matmul(ps[2 * g + c], gateT[:, g * T:(g + 1) * T], bdn[:, c * 512:(c + 1) * 512],
                                     start=True, stop=True)
            last.then_inc(s["yi_mm"], 1)
            pe.wait_ge(s["yi"], 4)
            pe.wait_ge(s["rank2"], 2)
            with pe.Fori(0, E // 2) as i:
                pe_pair(pe, 0, i)
            pe.wait_ge(s["flag"], 1)
            more = pe.value_load(most_i[0:1, 0:1], min_val=0, max_val=N)
            with pe.If(more > S):
                with pe.Fori(1, N // S) as turn:
                    with pe.Fori(0, E // 2) as i:
                        pe_pair(pe, turn * (E // 2), i)
            pe.wait_ge(s["gt2"], 1)
            spread(1, 2, 4).then_inc(s["gtb"], 1)

        def act_pair(a, base, i):
            n = base + i
            for b in range(2):
                a.wait_ge(s["gathered"], n * 2 + (b + 1))
                a.activation(xT[:, 4 * b:4 * b + 4, :].rearrange("p c s -> p (c s)"), ps[4 + b], ACT.Copy)\
                    .then_inc(s["xt_ready"], 1)
            for q in range(2):
                a.wait_ge(s["glu_ready"], n * 2 + (q + 1))
                a.activation(sig, glu, ACT.Sigmoid, scale=1.702).then_inc(s["sig_done"], 1)
                if q == 1:
                    a.wait_ge(s["gt_tr"], n + 1)
                    a.activation(GT.rearrange("p g t -> p (g t)"), ps[6][:, 0:N], ACT.Copy).then_inc(s["gt_ready"], 1)
                a.wait_ge(s["act_tr"], n * 2 + (q + 1))
                a.activation(actT.rearrange("p m t -> p (m t)"), ps[3], ACT.Copy).then_inc(s["actT_ready"], 1)
                a.wait_ge(s["dn_used"], n * 16 + KC * (q + 1))
                a.activation(outp[64 * q:64 * q + 64, 512:1024], ps[2][64:128, :], ACT.Copy).then_inc(s["outp_ready"], 1)

        @block.scalar
        def _(a):
            a_at = Steps()
            a.dma_start(const, const_in).then_inc(s["in_const"], 16)
            a.wait_ge(s["silu_pad"], 1)
            a.dma_start(siluT[:, :, 0:G], cond_in).then_inc(s["in_cond"], 16)
            a.dma_start(chan, chan_in).then_inc(s["in_const"], 16)
            a.dma_start(madd0, mod_in[0, :, 0:512]).then_inc(s["in_mod"], 16)
            a.dma_start(mmul0, mod_in[1, :, 0:512]).then_inc(s["in_mod"], 16)
            a.dma_start(level_f, level_in).then_inc(s["in_rw"], 16)
            a.wait_ge(s["in_x"], 16)
            for g in range(G):
                a.activation(junk0, x0[:, g, :], ACT.Square, accum_out=ssx[:, g:g + 1]).then_inc(s["a_step"], a_at.mark("ms_x"))
                a.wait_ge(s["a_step"], a_at.after("ms_x", g + 1))
            a.wait_ge(s["in_const"], 32)
            a.activation(rsx[:, 0:G], ssx[:, 0:G], ACT.Sqrt, scale=1.0 / D, bias=eps[0]).then_inc(s["rs_x"], 1)
            a.wait_ge(s["in_cond"], 16)
            a.activation(junk0[:, 0:KC * 32], siluT.rearrange("p k m -> p (k m)"), ACT.Sigmoid).then_inc(s["silu_sig"], 1)
            a.wait_ge(s["xT_tr"], KC)
            a.wait_ge(s["modT"], 1)
            for c in range(KC):
                hf, m = divmod(c, 4)
                a.activation(hT[:, c, 0:T], ps[1 + c // 4][:, (c % 4) * T:(c % 4 + 1) * T], ACT.Identity,
                             scale=modT[:, m, 32 * (2 + hf):32 * (2 + hf) + 1],
                             bias=modT[:, m, 32 * hf:32 * hf + 1]).then_inc(s["hT_a"], 1)
            for n, (kind, q, d, e) in enumerate(items):
                if e != "a":
                    continue
                out = bank_of(n)
                if n >= 19:
                    a.wait_ge(s["kv_mm"], n - 18)
                else:
                    a.wait_ge(s["l2_mm"], n + 1)
                if kind == "l1":
                    ins = a.activation(mids[:, q, :], out[:, 0:N], (ACT.Tanh, ACT.Copy, ACT.Sigmoid)[q])
                elif kind == "w":
                    ins = a.activation(sgw[:, 2 * q + d, :], out[:, 0:N], ACT.Sigmoid, bias=chan[:, q, C_W0 + d:C_W0 + d + 1])
                elif kind == "a":
                    ins = a.activation(aT[:, d, q, :], out[:, 0:N], ACT.Sigmoid, bias=chan[:, q, C_A0 + d:C_A0 + d + 1])
                elif kind == "k":
                    if q == 0:
                        a.wait_ge(s["level"], 1)
                    ins = a.activation(kT[:, q, :], out[:, 0:N], ACT.Copy)
                elif kind == "cg":
                    ins = a.activation(sgc[:, q, :], out[:, 0:N], ACT.Sigmoid)
                ins.then_inc(s["a_sig"], 1)
                if kind == "k":
                    a.wait_ge(s["a_sig"], emptied(n + 1, "a"))
                    a.wait_ge(s["kk_raw"], q + 1)
                    a.activation(sqk[:, q, :], kkT[:, q, :], ACT.Square).then_inc(s["kk_sq"], 1)
                if kind == "k" and q == Q - 1:
                    a.wait_ge(s["kk"], 2 * Q)
                    a.activation(rn.rearrange("p q t -> p (q t)"), rn.rearrange("p q t -> p (q t)"), ACT.Sqrt)\
                        .then_inc(s["kk_sqrt"], 1)
            for q in range(Q):
                def decays(r):
                    a.wait_ge(s["pre"], 8 * G)
                    if r > 0:
                        a.wait_ge(s["prep"], r)
                        a.wait_ge(s["prep_s"], r)
                    for sg, sc in enumerate((-KAPPA, KAPPA)):
                        last = a.activation(Ex[:, sg], Pc[:, :, r], ACT.Exp, scale=sc)
                    last.then_inc(s["ex"], 1)

                if q == 0:
                    a.wait_ge(s["scan"], 8 * G)
                    decays(0)
                a.wait_ge(s["bt_mm"], q + 1)
                a.activation(r_bk, ps[4], ACT.Copy).then_inc(s["bt_ev"], 1)
                for g in range(G):
                    a.wait_ge(s["w_mm"], 2 * q + g + 1)
                    a.activation(W[:, g].rearrange("p d i -> p (d i)"), ps[6 + g][:, 0:256], ACT.Copy)\
                        .then_inc(s["w_ev"], 1)
                for lv in range(1, LEVELS):
                    for g in range(G):
                        n = 12 * q + 2 * (lv - 1) + g + 1
                        a.wait_ge(s["p_mm"], n)
                        if n > 2:
                            a.wait_ge(s["e_mm"], n - 2)
                        a.activation(Pn[:, g].rearrange("p h d t -> p (h d t)"), ps[g], ACT.Copy).then_inc(s["p_ev"], 1)
                    if lv == 2 and q < Q - 1:
                        decays(q + 1)
                for g in range(G):
                    a.wait_ge(s["sa_mm"], 2 * q + g + 1)
                    a.activation(SA[:, g].rearrange("p d i -> p (d i)"), ps[6 + g][:, 256:512], ACT.Copy)\
                        .then_inc(s["sa_ev"], 1)
                for g in range(G):
                    a.wait_ge(s["y_mm"], 2 * q + g + 1)
                    a.activation(oT[:, q, g * T:(g + 1) * T], ps[g][:, 0:T], ACT.Copy).then_inc(s["o_ev"], 1)
                a.wait_ge(s["st_mm"], q + 1)
                for h in range(2):
                    a.activation(stS[HD * h:HD * h + HD, :, q, :],
                                 ps[2][HD * h:HD * h + HD, 0:256].rearrange("p (d j) -> p d j", d=2)[:, :, HD * h:HD * h + HD],
                                 ACT.Copy).then_inc(s["st_ev"], 1)
            for g in range(G):
                a.wait_ge(s["vt_mm"], g + 1)
                a.activation(vT[:, :, g * T:(g + 1) * T], ps[4 + g].rearrange("p (q t) -> p q t", q=Q), ACT.Copy)\
                    .then_inc(s["vt"], 1)
            for b in range(2):
                a.wait_ge(s["gt_mm"], b + 1)
                a.activation(gT[:, 2 * b:2 * b + 2, :].rearrange("p q t -> p (q t)"), ps[4 + b], ACT.Copy)\
                    .then_inc(s["gt"], 1)
            for b in range(2):
                a.wait_ge(s["gn_cen"], b + 1)
                a.activation(sq[:, 2 * b:2 * b + 2, :], oc[:, 2 * b:2 * b + 2, :], ACT.Square).then_inc(s["gn_sq"], 1)
            a.wait_ge(s["c_cen"], Q)
            a.activation(csq.rearrange("p q t -> p (q t)"), acc.rearrange("p q t -> p (q t)"), ACT.Square)\
                .then_inc(s["c_sq"], 1)
            for b in range(2):
                a.wait_ge(s["gv_mm"], b + 1)
                a.activation(sq[:, 2 * b:2 * b + 2, :].rearrange("p q t -> p (q t)"), ps[b], ACT.Sqrt,
                             scale=1.0 / HD, bias=eps[2]).then_inc(s["gn_std"], 1)
            a.wait_ge(s["cv_mm"], 1)
            a.activation(crs, ps[3][:, 0:A_COLS], ACT.Sqrt, scale=1.0 / CH, bias=eps[1]).then_inc(s["c_std"], 1)
            a.wait_ge(s["c_n2"], Q)
            a.activation(csg.rearrange("p q t -> p (q t)"), acc.rearrange("p q t -> p (q t)"), ACT.Sigmoid)\
                .then_inc(s["c_sig"], 1)
            for n in range(4):
                a.wait_ge(s["mix_mm"], n + 1)
                a.activation(junk[:, 512 * (n % 2):512 * (n % 2) + 512], ps[n], ACT.Square, accum_out=ssm[:, n:n + 1])\
                    .then_inc(s["mix_ss"], 1)
                a.wait_ge(s["mix_ss"], n + 1)
            a.wait_ge(s["mix_rs"], 1)
            a.activation(rsm[:, 0:G], rsm[:, 0:G], ACT.Sqrt, scale=1.0 / D, bias=eps[0]).then_inc(s["mix_rec"], 1)
            a.wait_ge(s["mix_rec"], 2)
            for n in range(4):
                g, c = divmod(n, 2)
                a.activation(mixn[:, g, c * 512:(c + 1) * 512], ps[n], ACT.Identity, scale=rsm[:, g:g + 1])\
                    .then_inc(s["mixn"], 1)
            for g in range(G):
                a.wait_ge(s["x1"], 2 * g + 2)
                a.activation(junk, x1[:, g, :], ACT.Square, accum_out=ss2[:, g:g + 1]).then_inc(s["a_step"], a_at.mark("ms_2"))
                a.wait_ge(s["a_step"], a_at.after("ms_2", g + 1))
            a.activation(rs2[:, 0:G], ss2[:, 0:G], ACT.Sqrt, scale=1.0 / D, bias=eps[0]).then_inc(s["rs_2"], 1)
            for n in range(4):
                g, b = divmod(n, 2)
                a.wait_ge(s["h2T_tr"], n + 1)
                a.activation(h2T[:, 4 * b:4 * b + 4, g * T:(g + 1) * T], ps[n].rearrange("p (c t) -> p c t", c=4), ACT.Copy)\
                    .then_inc(s["h2T"], 1)
            for g in range(G):
                a.wait_ge(s["negm"], g + 1)
                a.activation(ex[:, g, :], ext[:, g, 0:E], ACT.Exp, bias=negm[:, g:g + 1]).then_inc(s["expm"], 1)
            a.wait_ge(s["gT_tr"], 1)
            a.activation(gateT, ps[6][0:E, 0:N], ACT.Copy).then_inc(s["gT_ev"], 1)
            with a.Fori(0, E // 2) as i:
                act_pair(a, 0, i)
            a.wait_ge(s["flag"], 1)
            more = a.value_load(most_i[0:1, 0:1], min_val=0, max_val=N)
            with a.If(more > S):
                with a.Fori(1, N // S) as turn:
                    with a.Fori(0, E // 2) as i:
                        act_pair(a, turn * (E // 2), i)
            for g in range(G):
                a.wait_ge(s["gt2"], 1)
                a.activation(junk, yacc[:, g, :], ACT.Square, accum_out=ssm[:, g:g + 1]).then_inc(s["a_step"], a_at.mark("y_ss"))
                a.wait_ge(s["a_step"], a_at.after("y_ss", g + 1))
            a.activation(rsm[:, 0:G], ssm[:, 0:G], ACT.Sqrt, scale=1.0 / D, bias=eps[0]).then_inc(s["y_rs"], 1)

        @block.gpsimd
        def _(po):
            po_at = Steps()
            po.memset(siluT, 0.0).then_inc(s["silu_pad"], 1)
            po.memset(r_L[:, 3072:5120], 0.0).then_inc(s["pool_zero"], 1)
            po.memset(r_u, 0.0)
            po.memset(S0.rearrange("p w d j -> p (w d j)"), 0.0).then_inc(s["pool_zero"], 1)
            po.wait_ge(s["pool_zero"], 2)
            for r in range(2):
                for h in range(2):
                    po.dma_start(S0[HD * h:HD * h + HD, r, :, HD * h:HD * h + HD],
                                 s0_in[:, 2 * r + h].rearrange("d j i -> j d i")).then_inc(s["s0_in"], 16)
            po.wait_ge(s["in_rw"], 16)
            po.tensor_copy(level[:, :, 0:2, :], level_f)
            po.tensor_copy(level[:, :, 2, :], level_f[:, :, 0, :]).then_inc(s["level"], 1)
            po.wait_ge(s["l2_mm"], 19)
            po.wait_ge(s["level"], 1)
            for h in range(2):
                other = 1 - h
                last = po.memset(kbp[HD * other:HD * other + HD, :, :, h], 0.0)
            last.then_inc(s["pool_zero"], 1)
            po.wait_ge(s["in_const"], 32)
            po.wait_ge(s["pool_zero"], 3)
            po.tensor_scalar(omka, chan[:, :, C_KA], -1.0, 1.0, ALU.mult, ALU.add).then_inc(s["po_step"], po_at.mark("omka"))
            po.wait_ge(s["po_step"], po_at.after("omka", 1))
            for q in range(Q):
                w = q % 2
                if q == 0:
                    po.wait_ge(s["a_sig"], 23)
                    po.wait_ge(s["kk_mm"], 1)
                if q > 0:
                    po.wait_ge(s["prep"], q)
                po.tensor_scalar(kd, aT[:, :, q, :], chan[:, q, C_KA:C_KA + 1], omka[:, q:q + 1], ALU.mult, ALU.add)\
                    .then_inc(s["po_step"], po_at.mark("pool_t1"))
                po.wait_ge(s["po_step"], po_at.after("pool_t1", q + 1))
                po.tensor_tensor(kd, kd, kT[:, q, :].unsqueeze(1).broadcast_to([P, 2, N]), ALU.mult)
                po.tensor_tensor(bv, aT[:, :, q, :], kkT[:, q, :].unsqueeze(1).broadcast_to([P, 2, N]), ALU.mult)\
                    .then_inc(s["kdb"], 1)
                po.wait_ge(s["ex"], q + 1)
                po.wait_ge(s["s0_in"], 64 if q < 2 else 128)
                if q >= 2:
                    po.wait_ge(s["st_mm"], q - 1)
                for d in range(2):
                    po.tensor_scalar(dgm[:, w, d, :], ident, Ex[:, 0, d, 0, T:T + 1], None, ALU.mult)
                    last = po.tensor_scalar(S0s[:, w, d, :], S0[:, w, d, :], Ex[:, 0, d, 1, T:T + 1], None, ALU.mult)
                last.then_inc(s["prep_s"], 1)
                if q < 2:
                    po.wait_ge(s["prep_s"], q + 1)
                    for h in range(2):
                        po.dma_start(S0[HD * h:HD * h + HD, w, :, HD * h:HD * h + HD],
                                     s0_in[:, 2 * (q + 2) + h].rearrange("d j i -> j d i")).then_inc(s["s0_in"], 16)
                if q > 0:
                    po.wait_ge(s["sa_mm"], 2 * q)
                else:
                    po.wait_ge(s["kv_mm"], len(items) - 19)
                for g in range(G):
                    po.tensor_copy(X[:, g].rearrange("p h d t -> p (h d) t"), ident.unsqueeze(1).broadcast_to([P, 4, P]))
                    last = po.tensor_copy(Y[:, g].rearrange("p h d t -> p (h d) t"),
                                          ident.unsqueeze(1).broadcast_to([P, 4, P]))
                    last.then_inc(s["xy"], 1)
                po.wait_ge(s["kdb"], q + 1)
                po.tensor_tensor(rkk[:, q, :], kd[:, 0, :], kd[:, 1, :], ALU.add).then_inc(s["rsum"], 1)
                po.wait_ge(s["rsum"], 3 * q + 1)
                po.tensor_tensor(rkk[:, q, :], rkk[:, q, :], rT[:, q, :], ALU.mult).then_inc(s["rsum"], 1)
                po.wait_ge(s["rsum"], 3 * q + 2)
                po.tensor_scalar(rkk[:, q, :], rkk[:, q, :], chan[:, q, C_RK:C_RK + 1], None, ALU.mult)\
                    .then_inc(s["rsum"], 1)
                po.wait_ge(s["rsum"], 3 * q + 3)
            po.wait_ge(s["prep"], Q)
            po.wait_ge(s["prep_s"], Q)
            po.dma_start(rw, router_w.rearrange("(k p) e -> p k e", p=P)).then_inc(s["in_router"], 16)
            po.dma_start(rb, router_b.partition_broadcast(P)).then_inc(s["in_router"], 16)
            po.wait_ge(s["y_mm"], 2 * Q)
            po.dma_start(bgu, b_gu).then_inc(s["in_router"], 16)
            po.dma_start(bdn, b_down).then_inc(s["in_router"], 16)

        def dve_pair(v, base, i, turn=None):
            n = base + i
            if turn is not None:
                v.wait_ge(s["shifted"], turn)
            for q in range(2):
                for g in range(G):
                    v.tensor_scalar(sel[:, g, q, :], iota, rank[:, g, bass.ds(i * 2 + q, 1)], None, ALU.is_equal)
                    v.tensor_scalar(selg[:, g, q, :], iota, rank[:, g, bass.ds(i * 2 + q, 1)],
                                    gate[:, g, bass.ds(i * 2 + q, 1)], ALU.is_equal, ALU.mult)
                last = v.tensor_copy(bsel[:, q, :], ident[0:E, bass.ds(i * 2 + q, 1)].broadcast_to([E, S]))
            last.then_inc(s["sel_ready"], 1)
            for q in range(2):
                v.wait_ge(s["gu_used"], n * 16 + KC * (q + 1))
                v.tensor_scalar(glu, ps[0], 7.0, None, ALU.min).then_inc(s["glu_ready"], 1)
                v.tensor_scalar(lin, ps[1], 7.0, -7.0, ALU.min, ALU.max).then_inc(s["lin_ready"], 1)
                v.wait_ge(s["lin_ready"], n * 2 + (q + 1))
                v.scalar_tensor_tensor(lin, lin, 1.0, glu, ALU.add, ALU.mult).then_inc(s["act_tmp"], 1)
                v.wait_ge(s["act_tmp"], n * 2 + (q + 1))
                v.wait_ge(s["sig_done"], n * 2 + (q + 1))
                v.tensor_tensor(act, lin, sig, ALU.mult).then_inc(s["act_ready"], 1)
                v.wait_ge(s["dn_used"], n * 16 + KC * (q + 1))
                v.tensor_copy(outp[64 * q:64 * q + 64, 0:512], ps[2][0:64, :]).then_inc(s["outp_ready"], 1)
            for g in range(G):
                for c in range(2):
                    v.wait_ge(s["combined"], n * 4 + (2 * g + c + 1))
                    v.tensor_tensor(yacc[:, g, c * 512:(c + 1) * 512], yacc[:, g, c * 512:(c + 1) * 512],
                                    ps[4 + 2 * g + c], ALU.add).then_inc(s["y_added"], 1)
            v.wait_ge(s["y_added"], n * 4 + 4)

        @block.vector
        def _(v):
            v_at = Steps()
            v.wait_ge(s["rs_x"], 1)
            v.reciprocal(rsx[:, 0:G], rsx[:, 0:G]).then_inc(s["rs_x"], 1)
            v.wait_ge(s["rs_x"], 2)
            for g in range(G):
                v.tensor_scalar(xn[:, g, :], x0[:, g, :], rsx[:, g:g + 1], None, ALU.mult).then_inc(s["xn"], 1)
            v.wait_ge(s["silu_sig"], 1)
            v.tensor_tensor(siluT.rearrange("p k m -> p (k m)"), siluT.rearrange("p k m -> p (k m)"),
                            junk0[:, 0:KC * 32], ALU.mult).then_inc(s["silu"], 1)
            v.wait_ge(s["in_mod"], 32)
            v.wait_ge(s["ada0_acc"], KC)
            v.tensor_tensor(mod0, ps[0], madd0, ALU.add).then_inc(s["v_step"], v_at.mark("mod0_t"))
            v.wait_ge(s["v_step"], v_at.after("mod0_t", 1))
            v.scalar_tensor_tensor(mod0, mod0, const[:, K_ONE:K_ONE + 1], mmul0, ALU.add, ALU.mult).then_inc(s["mod0"], 1)
            v.wait_ge(s["mod0_tr"], 1)
            v.tensor_copy(modT.rearrange("p m r -> p (m r)"), ps[5]).then_inc(s["modT"], 1)
            v.wait_ge(s["modT"], 1)
            v.wait_ge(s["xT_tr"], KC)
            for c in range(KC):
                hf, m = divmod(c, 4)
                v.tensor_scalar(hT[:, c, T:N], ps[3 + c // 4][:, (c % 4) * T:(c % 4 + 1) * T],
                                modT[:, m, 32 * (2 + hf) + 1:32 * (2 + hf) + 2], modT[:, m, 32 * hf + 1:32 * hf + 2],
                                ALU.mult, ALU.add).then_inc(s["hT_v"], 1)
            for q in range(Q):
                for d in range(2):
                    n = 2 * q + d
                    v.wait_ge(s["a_sig"], 4 + n)
                    for g in range(G):
                        run = Pc[:, d, q, g, :]
                        v.memset(run[:, 0:1], 0.0)
                        v.tensor_tensor_scan(run[:, 1:T + 1], ones, sgw[:, n, g * T:(g + 1) * T], 0.0,
                                             ALU.mult, ALU.add).then_inc(s["scan"], 1)
                for d in range(2):
                    for g in range(G):
                        n = 4 * q + 2 * d + g
                        half = ssx[:, 0:1] if n % 2 == 0 else ssx[:, 1:2]
                        run = Pc[:, d, q, g, :]
                        v.wait_ge(s["scan"], n + 1)
                        if n >= 2:
                            v.wait_ge(s["pre"], n - 1)
                        v.tensor_scalar(half, run[:, T:T + 1], 0.5, None, ALU.mult).then_inc(s["v_step"], v_at.mark("sgw_used"))
                        v.wait_ge(s["v_step"], v_at.after("sgw_used", n + 1))
                        v.tensor_scalar(run, run, half, None, ALU.subtract).then_inc(s["pre"], 1)
            def take_k(q):
                v.wait_ge(s["a_sig"], 3 + 16 + q + 1)
                v.tensor_scalar(kkT[:, q, :], kT[:, q, :], chan[:, q, C_KK:C_KK + 1], None, ALU.mult).then_inc(s["kk_raw"], 1)

            for q in range(Q):
                take_k(q)
            for n, (kind, q, d, e) in enumerate(items):
                if e != "v":
                    continue
                out = bank_of(n)
                v.wait_ge(s["kv_mm"], n - 18)
                if kind == "r":
                    v.tensor_copy(rT[:, q, :], out[:, 0:N]).then_inc(s["kk"], 1)
                elif kind == "kn":
                    v.tensor_scalar(rn[:, q, :], out[:, 0:N], 1e-24, None, ALU.max).then_inc(s["kk"], 1)
                    if q == Q - 1:
                        v.wait_ge(s["kk_sqrt"], 1)
                        v.reciprocal(rn.rearrange("p q t -> p (q t)"), rn.rearrange("p q t -> p (q t)")).then_inc(s["v_step"], v_at.mark("kk_rec"))
                        v.wait_ge(s["v_step"], v_at.after("kk_rec", 1))
                        v.tensor_tensor(r_kk, r_kk, rn.rearrange("p q t -> p (q t)"), ALU.mult).then_inc(s["kk_mm"], 1)
                elif kind == "v":
                    v.tensor_copy(V[:, q, :], out).then_inc(s["kk"], 1)
                elif kind == "cv":
                    v.wait_ge(s["a_sig"], emptied(n + 1, "a"))
                    v.wait_ge(s["pool_zero"], 2)
                    v.tensor_tensor(u[:, q, U_CTX:U_CTX + T], out[:, 0:T], sgc[:, q, 0:T], ALU.mult)
                    v.tensor_tensor(u[:, q, U_LAT:U_LAT + 2 * U_STEP].rearrange("p (r c) -> p r c", r=2)[:, :, 0:SEG],
                                    out[:, T:N].rearrange("p (r c) -> p r c", r=2),
                                    sgc[:, q, T:N].rearrange("p (r c) -> p r c", r=2), ALU.mult).then_inc(s["kk"], 1)

            def prep(q):
                w = q % 2
                v.wait_ge(s["kdb"], q + 1)
                v.wait_ge(s["ex"], q + 1)
                if q == 0:
                    v.wait_ge(s["pool_zero"], 3)
                    v.wait_ge(s["kk_mm"], 1)
                else:
                    v.wait_ge(s["m_mm"], 8 * q)
                    v.wait_ge(s["bt_mm"], q)
                kk_q = kkT[:, q, :].rearrange("p (g t) -> p g t", g=G)
                r_q = rT[:, q, :].rearrange("p (g t) -> p g t", g=G)
                for d in range(2):
                    up, at_r, at_a = (0, 1, 0) if d == 0 else (1, 0, 1)
                    down, at_k = (1, 1) if d == 0 else (0, 0)
                    v.tensor_tensor(ra[:, w, :, d, 0, :], r_q, Ex[:, up, d, :, at_r:at_r + T], ALU.mult)
                    v.scalar_tensor_tensor(ra[:, w, :, d, 1, :], kk_q, -1.0, Ex[:, up, d, :, at_a:at_a + T], ALU.mult, ALU.mult)
                    for k, src in enumerate((kd, bv)):
                        for h in range(2):
                            half = slice(HD * h, HD * h + HD)
                            last = v.tensor_tensor(kbp[half, :, k, h, d, :], src[half, d, :].rearrange("p (g t) -> p g t", g=G),
                                                   Ex[half, down, d, :, at_k:at_k + T], ALU.mult)
                last.then_inc(s["prep"], 1)

            def conv_taps(n0, n1):
                for n in range(n0, min(n1, TAPS * Q)):
                    tap, q = divmod(n, Q)
                    wcol = chan[:, q, tap:tap + 1]
                    if tap == 0:
                        v.tensor_scalar(acc[:, q, :], u[:, q, 0:A_COLS], wcol, chan[:, q, C_CONVB:C_CONVB + 1],
                                        ALU.mult, ALU.add).then_inc(s["conv"], 1)
                    else:
                        v.wait_ge(s["conv"], n - Q + 1)
                        v.scalar_tensor_tensor(acc[:, q, :], u[:, q, tap:tap + A_COLS], wcol, acc[:, q, :],
                                               ALU.mult, ALU.add).then_inc(s["conv"], 1)

            def level_mask(lv, swap):
                return level[:, lv, swap:swap + 2, :].unsqueeze(1).broadcast_to([P, 2, 2, T])

            prep(0)
            v.wait_ge(s["kk"], emptied(len(items), "v"))
            for q in range(Q):
                for g in range(G):
                    for i in range(4):
                        h, d = divmod(i, 2)
                        n = 8 * q + 4 * g + i
                        v.wait_ge(s["m_mm"], n + 1)
                        v.tensor_tensor(LT[:, g, h, d].rearrange("p (k a) t -> p k a t", k=2),
                                        ps[6 + n % 2].rearrange("p (k a t) -> p k a t", k=2, a=2),
                                        mask_lt[:, d].unsqueeze(1).broadcast_to([P, 2, 2, T]), ALU.mult)\
                            .then_inc(s["m_ev"], 1)
                v.wait_ge(s["level"], 1)
                for lv in range(LEVELS):
                    conv_taps(5 * (7 * q + lv), 5 * (7 * q + lv) + 5)
                    if lv == 0:
                        v.wait_ge(s["m_ev"], 8 * q + 8)
                    for g in range(G):
                        if lv == 0:
                            v.wait_ge(s["xy"], 2 * q + g + 1)
                        if lv < LEVELS - 1:
                            v.wait_ge(s["d_mm"], 12 * q + 2 * lv + g + 1)
                            v.copy_predicated(X[:, g], level_mask(lv, 0),
                                              ps[2 + 2 * g].rearrange("p (h d t) -> p h d t", h=2, d=2)).then_inc(s["x_up"], 1)
                        if lv == 0:
                            v.copy_predicated(Y[:, g], level_mask(lv, 1), LT[:, g, :, :, 3, :]).then_inc(s["y_up"], 1)
                        else:
                            v.wait_ge(s["e_mm"], 12 * q + 2 * (lv - 1) + g + 1)
                            v.copy_predicated(Y[:, g], level_mask(lv, 1),
                                              ps[3 + 2 * g].rearrange("p (h d t) -> p h d t", h=2, d=2)).then_inc(s["y_up"], 1)
                    if lv == 3 and q < Q - 1:
                        prep(q + 1)
                v.wait_ge(s["ada_acc"], 4 * (q + 1))
                b = q // 2
                if q == 0:
                    v.wait_ge(s["in_mod"], 64)
                v.tensor_tensor(mod[:, b, :], ps[6], madd[:, b, :] if q % 2 == 0 else mod[:, b, :], ALU.add)\
                    .then_inc(s["mod_t"], 1)
                if q % 2:
                    v.wait_ge(s["mod_t"], q + 1)
                    v.scalar_tensor_tensor(mod[:, b, :], mod[:, b, :], const[:, K_ONE + 1 + b:K_ONE + 2 + b], mmul[:, b, :],
                                           ALU.add, ALU.mult).then_inc(s["mod"], 1)
            for b in range(2):
                v.wait_ge(s["gn_mm"], b + 1)
                if b == 0:
                    v.wait_ge(s["o_ev"], 2 * Q)
                v.scalar_tensor_tensor(oc[:, 2 * b:2 * b + 2, :], ps[b].rearrange("p (q t) -> p q t", q=2), -1.0 / HD,
                                       oT[:, 2 * b:2 * b + 2, :], ALU.mult, ALU.add).then_inc(s["gn_cen"], 1)
            v.wait_ge(s["cm_mm"], 1)
            for q in range(Q):
                v.scalar_tensor_tensor(acc[:, q, :], ps[3][:, 0:A_COLS], -1.0 / CH, acc[:, q, :], ALU.mult, ALU.add)\
                    .then_inc(s["c_cen"], 1)
            v.wait_ge(s["vt"], 2)
            for b in range(2):
                v.wait_ge(s["bo_mm"], b + 1)
                v.tensor_tensor(rkk[:, 2 * b:2 * b + 2, :], ps[(2, 7)[b]].rearrange("p (q t) -> p q t", q=2),
                                vT[:, 2 * b:2 * b + 2, :], ALU.mult).then_inc(s["bo"], 1)
            for b in range(2):
                two = slice(2 * b, 2 * b + 2)
                v.wait_ge(s["gn_std"], b + 1)
                v.reciprocal(sq[:, two, :], sq[:, two, :]).then_inc(s["v_step"], v_at.mark("gn_rec"))
                v.wait_ge(s["v_step"], v_at.after("gn_rec", b + 1))
                v.tensor_tensor(oc[:, two, :], oc[:, two, :], sq[:, two, :], ALU.mult).then_inc(s["v_step"], v_at.mark("gn_1"))
                v.wait_ge(s["v_step"], v_at.after("gn_1", b + 1))
                for q in (2 * b, 2 * b + 1):
                    v.tensor_scalar(oc[:, q, :], oc[:, q, :], chan[:, q, C_GNG:C_GNG + 1], chan[:, q, C_GNB:C_GNB + 1],
                                    ALU.mult, ALU.add).then_inc(s["v_step"], v_at.mark("gn_2"))
                v.wait_ge(s["v_step"], v_at.after("gn_2", 2 * b + 2))
                v.wait_ge(s["bo"], b + 1)
                v.tensor_tensor(oc[:, two, :], oc[:, two, :], rkk[:, two, :], ALU.add).then_inc(s["v_step"], v_at.mark("gn_3"))
                v.wait_ge(s["v_step"], v_at.after("gn_3", b + 1))
                v.wait_ge(s["gt"], b + 1)
                v.tensor_tensor(oT[:, two, :], oc[:, two, :], gT[:, two, :], ALU.mult).then_inc(s["gn_out"], 1)
            v.wait_ge(s["c_std"], 1)
            v.reciprocal(crs, crs).then_inc(s["v_step"], v_at.mark("c_rec"))
            v.wait_ge(s["v_step"], v_at.after("c_rec", 1))
            v.wait_ge(s["c_sq"], 1)
            for q in range(Q):
                v.tensor_tensor(acc[:, q, :], acc[:, q, :], crs, ALU.mult).then_inc(s["v_step"], v_at.mark("c_n1"))
            for q in range(Q):
                v.wait_ge(s["v_step"], v_at.after("c_n1", q + 1))
                v.tensor_scalar(acc[:, q, :], acc[:, q, :], chan[:, q, C_LNG:C_LNG + 1], chan[:, q, C_LNB:C_LNB + 1],
                                ALU.mult, ALU.add).then_inc(s["c_n2"], 1)
            v.wait_ge(s["c_sig"], 1)
            for q in range(Q):
                v.tensor_tensor(cvT[:, q, 0:T], acc[:, q, 0:T], csg[:, q, 0:T], ALU.mult)
                lat = slice(A_LAT, A_LAT + SEG + U_STEP)
                for r in range(2):
                    c0 = A_LAT + r * U_STEP
                    last = v.tensor_tensor(cvT[:, q, T + SEG * r:T + SEG * r + SEG], acc[:, q, c0:c0 + SEG],
                                           csg[:, q, c0:c0 + SEG], ALU.mult)
                last.then_inc(s["c_out"], 1)
            v.wait_ge(s["mix_ss"], 4)
            for g in range(G):
                last = v.tensor_tensor(rsm[:, g:g + 1], ssm[:, 2 * g:2 * g + 1], ssm[:, 2 * g + 1:2 * g + 2], ALU.add)
            last.then_inc(s["mix_rs"], 1)
            v.wait_ge(s["mix_rec"], 1)
            v.reciprocal(rsm[:, 0:G], rsm[:, 0:G]).then_inc(s["mix_rec"], 1)
            v.wait_ge(s["gtb"], 1)
            v.wait_ge(s["in_x1"], 16)
            for n in range(4):
                g, c = divmod(n, 2)
                cols = slice(c * 512, (c + 1) * 512)
                v.wait_ge(s["mixn"], n + 1)
                v.tensor_tensor(mixn[:, g, cols], mixn[:, g, cols], ps[4 + n], ALU.mult).then_inc(s["mul1"], 1)
                v.wait_ge(s["mul1"], n + 1)
                v.tensor_tensor(x1[:, g, cols], x1[:, g, cols], mixn[:, g, cols], ALU.add).then_inc(s["x1"], 1)
            v.wait_ge(s["rs_2"], 1)
            v.reciprocal(rs2[:, 0:G], rs2[:, 0:G]).then_inc(s["v_step"], v_at.mark("rec_2"))
            v.wait_ge(s["v_step"], v_at.after("rec_2", 1))
            v.wait_ge(s["a2b"], 1)
            for n in range(4):
                g, c = divmod(n, 2)
                cols = slice(c * 512, (c + 1) * 512)
                v.scalar_tensor_tensor(h2[:, g, cols], x1[:, g, cols], rs2[:, g:g + 1], ps[n], ALU.mult, ALU.mult)\
                    .then_inc(s["v_step"], v_at.mark("h2_1"))
            v.wait_ge(s["b2b"], 1)
            for n in range(4):
                g, c = divmod(n, 2)
                cols = slice(c * 512, (c + 1) * 512)
                v.wait_ge(s["v_step"], v_at.after("h2_1", n + 1))
                v.tensor_tensor(h2[:, g, cols], h2[:, g, cols], ps[4 + n], ALU.add).then_inc(s["h2"], 1)
            v.memset(ext[:, :, E:40], -BIG)
            v.memset(b8[:, :, :], -BIG).then_inc(s["v_step"], v_at.mark("ext0"))
            v.wait_ge(s["in_router"], 64)
            v.wait_ge(s["logits"], 1)
            for g in range(G):
                v.tensor_tensor(ext[:, g, 0:E], ps[4][:, g * E:(g + 1) * E], rb, ALU.add).then_inc(s["v_step"], v_at.mark("lg"))
            v.wait_ge(s["v_step"], v_at.after("ext0", 1))
            for g in range(G):
                v.wait_ge(s["v_step"], v_at.after("lg", g + 1))
                v.max(m8[:, g, :], ext[:, g, 0:E]).then_inc(s["v_step"], v_at.mark("t8"))
            for g in range(G):
                v.wait_ge(s["v_step"], v_at.after("t8", g + 1))
                v.tensor_copy(b8[:, g, 0:TOPK], m8[:, g, 0:TOPK]).then_inc(s["v_step"], v_at.mark("b8"))
                v.tensor_scalar(negm[:, g:g + 1], m8[:, g, 0:1], -1.0, None, ALU.mult).then_inc(s["negm"], 1)
                v.wait_ge(s["v_step"], v_at.after("b8", g + 1))
                v.match_replace(rep[:, g, :], b8[:, g, :], ext[:, g, :], BIG).then_inc(s["v_step"], v_at.mark("rep"))
            for g in range(G):
                v.wait_ge(s["v_step"], v_at.after("rep", g + 1))
                v.tensor_tensor(sel_m[:, g, :], rep[:, g, 0:E], ext[:, g, 0:E], ALU.not_equal).then_inc(s["selm"], 1)
            for g in range(G):
                v.wait_ge(s["selm"], g + 1)
                v.wait_ge(s["expm"], g + 1)
                v.tensor_tensor(ex[:, g, :], ex[:, g, :], sel_m[:, g, :], ALU.mult).then_inc(s["v_step"], v_at.mark("exm"))
                v.wait_ge(s["v_step"], v_at.after("exm", g + 1))
                v.reduce_sum(gsum[:, g:g + 1], ex[:, g, :], AX.X).then_inc(s["v_step"], v_at.mark("gsum"))
                v.wait_ge(s["v_step"], v_at.after("gsum", g + 1))
                v.reciprocal(grec[:, g:g + 1], gsum[:, g:g + 1]).then_inc(s["v_step"], v_at.mark("grec"))
                v.wait_ge(s["v_step"], v_at.after("grec", g + 1))
                v.tensor_scalar(gate[:, g, :], ex[:, g, :], grec[:, g:g + 1], None, ALU.mult).then_inc(s["gate"], 1)
            v.wait_ge(s["rk_mm"], 1)
            for g in range(G):
                v.scalar_tensor_tensor(rank[:, g, :], ps[5][:, g * E:(g + 1) * E], 1.0, sel_m[:, g, :], ALU.add, ALU.mult)\
                    .then_inc(s["v_step"], v_at.mark("rank1"))
            for g in range(G):
                v.wait_ge(s["v_step"], v_at.after("rank1", g + 1))
                v.tensor_scalar(rank[:, g, :], rank[:, g, :], -1.0, None, ALU.add).then_inc(s["rank2"], 1)
            v.reduce_max(most, ps[5][:, 2 * E:3 * E], AX.X).then_inc(s["v_step"], v_at.mark("cnt"))
            v.wait_ge(s["v_step"], v_at.after("cnt", 1))
            v.tensor_copy(most_i, most).then_inc(s["flag"], 1)
            v.wait_ge(s["yi_mm"], 1)
            for n in range(4):
                g, c = divmod(n, 2)
                v.tensor_copy(yacc[:, g, c * 512:(c + 1) * 512], ps[n]).then_inc(s["yi"], 1)
            v.wait_ge(s["yi"], 4)
            v.wait_ge(s["rank2"], 2)
            with v.Fori(0, E // 2) as i:
                dve_pair(v, 0, i)
            v.wait_ge(s["flag"], 1)
            more = v.value_load(most_i[0:1, 0:1], min_val=0, max_val=N)
            with v.If(more > S):
                with v.Fori(1, N // S) as turn:
                    v.tensor_scalar(rank.rearrange("p g e -> p (g e)"), rank.rearrange("p g e -> p (g e)"),
                                    -float(S), None, ALU.add).then_inc(s["shifted"], 1)
                    with v.Fori(0, E // 2) as i:
                        dve_pair(v, turn * (E // 2), i, turn)
            v.tensor_copy(ss2[:, 0:1], eps[0]).then_inc(s["gt2"], 1)
            v.wait_ge(s["y_rs"], 1)
            v.reciprocal(rsm[:, 0:G], rsm[:, 0:G]).then_inc(s["v_step"], v_at.mark("y_rec"))
            v.wait_ge(s["v_step"], v_at.after("y_rec", 1))
            v.wait_ge(s["gtb"], 2)
            for n in range(4):
                g, c = divmod(n, 2)
                cols = slice(c * 512, (c + 1) * 512)
                v.scalar_tensor_tensor(yacc[:, g, cols], yacc[:, g, cols], rsm[:, g:g + 1], ps[4 + n], ALU.mult, ALU.mult)\
                    .then_inc(s["v_step"], v_at.mark("fin1"))
                v.wait_ge(s["v_step"], v_at.after("fin1", n + 1))
                v.tensor_tensor(x1[:, g, cols], x1[:, g, cols], yacc[:, g, cols], ALU.add).then_inc(s["fin"], 1)


def constants():
    c = np.zeros((P, K_N), np.float32)
    i = np.arange(P)
    c[:, K_ID:K_ID + P] = np.eye(P)
    c[:, K_HEAD:K_HEAD + P] = (i[:, None] // HD) == (i[None, :] // HD)
    c[:, K_ONES:K_ONES + P] = 1.0
    c[:, K_UPPER:K_UPPER + P] = i[:, None] < i[None, :]
    m = np.stack([np.stack([i[:, None] <= i[None, :], i[:, None] < i[None, :]], 1),
                  np.stack([i[:, None] >= i[None, :], i[:, None] > i[None, :]], 1)], 1)
    c[:, K_MASK:K_MASK + 512] = m.reshape(P, 512)
    c[:, K_IOTA:K_IOTA + S] = np.arange(S)
    c[:, K_EPS:K_EPS + 3] = (1e-6, 1e-5, 64e-5)
    for cc in (2, 3, 8, 9):
        b, j = divmod(cc, 4)
        c[32 * j:32 * j + G, K_ONE + b] = 1.0
    lv = np.zeros((P, LEVELS, 2, T), np.float32)
    for n in range(LEVELS):
        b = 1 << n
        low = (i[:, None] // b % 2 == 1) & (i[:, None] // b == i[None, :] // b + 1)
        lv[:, n, 0], lv[:, n, 1] = low, low.T
    return c, lv


def kernel(**inputs):
    import concourse.bacc as _bacc
    from concourse.bass_utils import run_bass_kernel_spmd as _run

    inp = {k: np.asarray(v) for k, v in inputs.items()}
    L = {k: inp[k][0] for k in inp if k not in ("x_prompt", "x_sample", "c", "c_ctx", "state_wkv_fwd", "state_wkv_bwd")}
    const, lv = constants()

    def chan_cols(v):
        return v.reshape(-1, Q, P).transpose(2, 1, 0)

    mod = np.zeros((2, P, 3 * 512), np.float32)
    rows = {0: L["ada_b"].reshape(12, 512)}
    gains = np.ones((12, 512), np.float32)
    for at, name in ((2, "pre_mix_g"), (4, "post_mix_g"), (8, "pre_ffn_g"), (10, "post_ffn_g")):
        gains[at:at + 2] = L[name].reshape(2, 512)
    rows[1] = gains
    for n in range(2):
        for cc in range(12):
            b, j = divmod(cc, 4)
            mod[n, 32 * j:32 * j + G, b * 512:(b + 1) * 512] = rows[n][cc]
    arrays = {
        "x": np.concatenate([inp["x_prompt"][0], inp["x_sample"][0]]),
        "cond": np.stack([inp["c_ctx"], inp["c"][0]]).reshape(G, KC, P).transpose(2, 1, 0),
        "ada_w": L["ada_w"], "mod": mod, "w_in": L["w_in"], "w_out": L["w_out"],
        "chan": np.concatenate([chan_cols(L[n].reshape(-1, CH)) for n in (
            "conv_w", "conv_b", "conv_ln_g", "conv_ln_b", "rw_w0", "rw_a0", "rw_k_k", "rw_k_a", "rw_r_k",
            "rw_gn_g", "rw_gn_b")], axis=2),
        "lora1": np.concatenate([L["rw_w1"][0], L["rw_w1"][1], L["rw_a1"][0], L["rw_a1"][1], L["rw_g1"]], axis=1)
        .reshape(KC, P, 3 * P).transpose(1, 0, 2),
        "w2": L["rw_w2"], "a2": L["rw_a2"], "g2": L["rw_g2"],
        "s0": np.stack([inp["state_wkv_fwd"][0, 0], inp["state_wkv_bwd"][0, 0]]).transpose(0, 1, 3, 2),
        "router_w": L["router_w"], "router_b": L["router_b"],
        "w_gu": L["w_gu"], "b_gu": L["b_gu"], "w_down": L["w_down"], "b_down": L["b_down"],
        "const": const, "level": lv,
    }
    nc = _bacc.Bacc("TRN2", target_bir_lowering=False, num_devices=1)
    args, feed = [], {}
    for name, a in arrays.items():
        a = np.ascontiguousarray(a)
        feed[f"in_{name}"] = a
        args.append(nc.dram_tensor(f"in_{name}", a.shape, mybir.dt.from_np(a.dtype), kind="ExternalInput").ap())
    outs = [("y_prompt", (T, D)), ("y_sample", (T, D)), ("st_f", (8, HD, HD)), ("st_b", (8, HD, HD))]
    for name, shape in outs:
        args.append(nc.dram_tensor(name, shape, FP32, kind="ExternalOutput").ap())
    build(nc, *args)
    r = _run(nc, [feed], core_ids=[0]).results[0]
    return (r["y_prompt"].reshape(1, T, D), r["y_sample"].reshape(1, T, D),
            r["st_f"].reshape(1, 1, 8, HD, HD), r["st_b"].reshape(1, 1, 8, HD, HD))
```

```python
import math
from contextlib import ExitStack

import numpy as np
import concourse.bass as bass
from concourse import mybir

FP32 = mybir.dt.float32
U8 = mybir.dt.uint8
I32 = mybir.dt.int32
ALU = mybir.AluOpType
ACT = mybir.ActivationFunctionType
AX = mybir.AxisListType

P = 128
G = 2
D = 1024
KC = D // P
T = 128
N = G * T
CH = 512
Q = CH // P
HD = 64
TAPS = 31
PAD = TAPS // 2
SEG = 64
LORA = 64
E = 32
TOPK = 4
F = 1024
S = 64
KAPPA = math.exp(-0.5)
LEVELS = 7
U_CTX, U_LAT = PAD, PAD + T + PAD
U_STEP = SEG + PAD
U_COLS = U_LAT + 2 * U_STEP
A_COLS = U_COLS - 2 * PAD
A_LAT = U_LAT - PAD
C_CONVB, C_LNG, C_LNB = TAPS, TAPS + 1, TAPS + 2
C_W0, C_A0 = TAPS + 3, TAPS + 5
C_KK, C_KA, C_RK, C_GNG, C_GNB = (TAPS + 7 + n for n in range(5))
C_N = TAPS + 12
K_ID, K_HEAD, K_ONES, K_UPPER, K_MASK, K_IOTA = 0, 128, 256, 384, 512, 1024
K_EPS = K_IOTA + S
K_ONE = K_EPS + 3
K_N = K_ONE + 3
BIG = 3.0e38
TAPS_U, TAPS_K, TAPS_R, TAPS_BEFORE, TAPS_BESIDE = (12, 16, 16), 8, 5, 3, (1, 1, 1)


def tap_order():
    order, done, latest = [], [0] * Q, [None] * Q
    while len(order) < TAPS * Q:
        there = 1 + sum(len(order) >= sum(TAPS_U[:n + 1]) for n in range(3))
        open_ = [c for c in range(there) if done[c] < TAPS]
        other = [c for c in open_ if not order or order[-1][0] != c]
        c = (other or open_)[0]
        order.append((c, done[c], latest[c]))
        latest[c] = len(order)
        done[c] += 1
    return order


FRONT = 28076


class Steps:

    def __init__(self):
        self.count, self.values = 0, {}

    def mark(self, name):
        self.count += 1
        self.values.setdefault(name, []).append(self.count)
        return 1

    def after(self, name, n):
        return self.values[name][n - 1]


def build(nc, x_in, cond_in, ada_w, mod_in, w_in, w_out, chan_in, lora1_in, w2_in, a2_in, g2_in,
          s0_in, router_w, router_b, w_gu, b_gu, w_down, b_down, const_in, level_in, part_in,
          y_prompt, y_sample, st_f, st_b):
    with ExitStack() as ctx:
        def sem(name):
            return ctx.enter_context(nc.semaphore(name))

        ring = ctx.enter_context(nc.sbuf_tensor("ring", [P, 24576], FP32))
        front = ctx.enter_context(nc.sbuf_tensor("front", [P, FRONT], FP32))
        level = ctx.enter_context(nc.sbuf_tensor("level", [P, LEVELS, 2, T], U8))
        ps = [ctx.enter_context(nc.psum_tensor(f"bank{n}", [P, 512], FP32))[:, :] for n in range(8)]
        top = [0]

        def take(words):
            top[0] += words
            assert top[0] <= FRONT, top[0]
            return front[:, top[0] - words:top[0]]

        def view(ap, pattern, **sizes):
            return ap.rearrange(pattern, **sizes)

        const = take(K_N)
        chan = view(take(Q * C_N), "p (q c) -> p q c", q=Q)
        r_hT, r_V, r_rk, r_kk = take(2048), take(1024), take(2048), take(1024)
        r_r, r_k = r_rk[:, 0:1024], r_rk[:, 1024:2048]
        r_a, r_P = take(2048), take(2 * Q * G * (T + 1))
        r_o, r_u = take(1024), take(Q * U_COLS)
        r_L = take(5240)
        g2 = take(512)
        r_mid = take(128 + 768)
        r_ra, r_E, r_kb, r_S0 = take(2048), take(1032), take(1024), take(512)
        r_mod = take(1024)
        siluT = view(take(KC * 32), "p (k m) -> p k m", k=KC)
        r_bk, r_S = take(512), take(512)
        small = take(248)

        ident = const[:, K_ID:K_ID + P]
        head_ones = const[:, K_HEAD:K_HEAD + P]
        ones = const[:, K_ONES:K_ONES + P]
        upper = const[:, K_UPPER:K_UPPER + P]
        mask_lt = view(const[:, K_MASK:K_MASK + 512], "p (d a t) -> p d a t", d=2, a=2)
        iota = const[:, K_IOTA:K_IOTA + S]
        eps = [const[:, K_EPS + n:K_EPS + n + 1] for n in range(3)]

        ada0 = view(ring[:, 0:16384], "p (k n) -> p k n", k=KC)
        x0 = view(r_P[:, 0:2048], "p (g d) -> p g d", g=G)
        xn = view(r_a, "p (g d) -> p g d", g=G)
        modT = view(r_kb[:, 0:512], "p (m r) -> p m r", m=4)
        mod0 = r_E[:, 0:512]
        madd0, mmul0 = r_ra[:, 0:512], r_ra[:, 512:1024]
        madd, mmul = (view(r_hT[:, 1024 * n:1024 * (n + 1)], "p (b n) -> p b n", b=2) for n in range(2))
        mod = view(r_mod, "p (b n) -> p b n", b=2)
        hT = view(r_hT, "p (c t) -> p c t", c=KC)
        level_f = view(r_rk[:, 0:LEVELS * 2 * T], "p (n a t) -> p n a t", n=LEVELS, a=2)
        win_cols = {"cg": CH, "cv": 0, "k": 3 * CH, "r": 2 * CH, "v": 4 * CH}
        win = {kind: view(ring[:, a:a + 4096], "p (k n) -> p k n", k=KC)
               for kind, a in zip(win_cols, (16384, 20480, 0, 4096, 8192))}
        lora1 = view(r_L[:, 0:3072], "p (k r) -> p k r", k=KC)
        w2p = view(r_L[:, 3072:4096], "p (d n) -> p d n", d=2)
        a2p = view(r_L[:, 4096:5120], "p (d n) -> p d n", d=2)
        mids = view(r_mid[:, 128:], "p (a t) -> p a t", a=3)
        sgw = view(r_ra, "p (n t) -> p n t", n=8)
        V = view(r_V, "p (g n) -> p g n", g=G)
        rT, kT, kkT = (view(a, "p (q t) -> p q t", q=Q) for a in (r_r, r_k, r_kk))
        aT = view(r_a, "p (d q t) -> p d q t", d=2, q=Q)
        Pc = view(r_P, "p (d q g t) -> p d q g t", d=2, q=Q, g=G)
        sgc = view(r_o, "p (q t) -> p q t", q=Q)
        u = view(r_u, "p (q t) -> p q t", q=Q)
        kbp = view(r_L[:, 0:2048], "p (g k h d t) -> p g k h d t", g=G, k=2, h=2, d=2)
        dgm = view(r_L[:, 2048:2560], "p (w d j) -> p w d j", w=2, d=2)
        S0s = view(r_L[:, 2560:3072], "p (w d j) -> p w d j", w=2, d=2)
        acc = view(r_L[:, 3072:3072 + Q * A_COLS], "p (q t) -> p q t", q=Q)
        rkk = view(r_L[:, 4216:5240], "p (q t) -> p q t", q=Q)
        sqk, rn = rkk, view(r_ra[:, 1024:2048], "p (q t) -> p q t", q=Q)
        ra = view(r_ra, "p (w g d k t) -> p w g d k t", w=2, g=G, d=2, k=2)
        Ex = view(r_E, "p (s d g t) -> p s d g t", s=2, d=2, g=G)
        kd = view(r_kb[:, 0:512], "p (d t) -> p d t", d=2)
        bv = view(r_kb[:, 512:1024], "p (d t) -> p d t", d=2)
        S0 = view(r_S0, "p (w d j) -> p w d j", w=2, d=2)
        bkT = view(r_bk, "p (k d j) -> p k d j", k=2, d=2)
        stS = view(r_S, "p (d q j) -> p d q j", d=2, q=Q)
        oT = view(r_o, "p (q t) -> p q t", q=Q)
        LT = view(ring[:, 16384:20480], "p (g h d k t) -> p g h d k t", g=G, h=2, d=2, k=4)
        X = view(ring[:, 20480:21504], "p (g c h t) -> p g c h t", g=G, c=2, h=2)
        Y = view(ring[:, 21504:23040], "p (g c h t) -> p g c h t", g=G, c=3, h=2)
        Pn = view(ring[:, 23040:23552], "p (g h t) -> p g h t", g=G, h=2)
        part_mask = view(r_mid[:, 0:(LEVELS - 2) * T], "p (n t) -> p n t", n=LEVELS - 2)
        W, SA = (view(ring[:, 23552 + 512 * n:24064 + 512 * n], "p (g d i) -> p g d i", g=G, d=2)
                 for n in range(2))
        ada_slot = view(ring[:, 0:8192], "p (k n) -> p k n", k=4)
        wout = view(ring[:, 8192:16384], "p (k n) -> p k n", k=KC)
        oc, sq = aT[:, 0], aT[:, 1]
        vT, gT = kT, kkT
        csq = view(r_u[:, 0:Q * A_COLS], "p (q t) -> p q t", q=Q)
        csg = view(r_L[:, 0:Q * A_COLS], "p (q t) -> p q t", q=Q)
        crs = r_L[:, 1200:1200 + A_COLS]
        cvT = view(r_E[:, 0:1024], "p (q t) -> p q t", q=Q)
        gtb = view(r_hT, "p (n d) -> p n d", n=4)
        mixn = view(r_a, "p (g d) -> p g d", g=G)
        x1 = view(r_P[:, 0:2048], "p (g d) -> p g d", g=G)
        h2 = view(r_L[:, 0:2048], "p (g d) -> p g d", g=G)
        h2T = hT
        scaled = h2
        rw = view(r_S0[:, 0:256], "p (k e) -> p k e", k=KC)
        rb = r_S0[:, 256:256 + E]
        wgu = view(ring[:, 0:16384], "p (k n) -> p k n", k=KC)
        wdn = view(ring[:, 16384:24576], "p (k n) -> p k n", k=KC)
        bgu = r_ra[0:E, :]
        bdn = r_kb[0:E, :]
        sel = view(r_E[:, 0:256], "p (g q s) -> p g q s", g=G, q=2)
        selg = view(r_E[:, 256:512], "p (g q s) -> p g q s", g=G, q=2)
        bsel = view(r_E[0:E, 512:640], "p (q s) -> p q s", q=2)
        GT = view(r_E[:, 640:896], "p (g t) -> p g t", g=G)
        xT = view(r_V, "p (c s) -> p c s", c=KC)
        glu, lin = r_r[:, 0:512], r_r[:, 512:1024]
        sig, act = r_k[:, 0:512], r_k[:, 512:1024]
        actT = view(r_kk[:, 0:512], "p (m s) -> p m s", m=4)
        outp = r_o
        yacc = view(r_a, "p (g d) -> p g d", g=G)
        junk0, junk = r_o, r_u[:, 0:1024]
        at = [0]

        def tiny(n):
            at[0] += n
            assert at[0] <= 248
            return small[:, at[0] - n:at[0]]

        ssx, rsx, ssm, rsm, ss2, rs2 = (tiny(4) for _ in range(6))
        omka = tiny(Q)
        ext = view(tiny(G * 40), "p (g e) -> p g e", g=G)
        m8 = view(r_bk[:, 0:16], "p (g e) -> p g e", g=G)
        b8 = view(r_bk[:, 16:32], "p (g e) -> p g e", g=G)
        rep = view(r_bk[:, 32:112], "p (g e) -> p g e", g=G)
        sel_m = view(r_bk[:, 112:176], "p (g e) -> p g e", g=G)
        ex = view(r_bk[:, 176:240], "p (g e) -> p g e", g=G)
        gsum = r_bk[:, 240:242]
        grec = r_bk[:, 242:244]
        negm = r_bk[:, 244:246]
        most = r_bk[:, 246:247]
        gate = view(tiny(G * (E + 2)), "p (g e) -> p g e", g=G)
        rank = view(tiny(G * (E + 2)), "p (g e) -> p g e", g=G)
        most_i = tiny(1).bitcast(I32)

        names = """level in_x in_const in_cond in_mod in_lora in_rw in_wout in_x1 in_router stored silu_pad
            silu_sig silu rs_x xn xT_tr ada0_acc mod0 mod0_tr modT hT_a hT_v l2_mm pre scan a_sig pool_zero
            kv_mm kk_raw kk_sq kk_mm kk_sqrt kk ex kdb prep_s prep s0_in rsum m_mm m_ev bt_mm bt_ev xy d_mm
            x_up y_up p_mm p_ev e_mm w_mm w_ev sa_mm sa_ev y_mm o_ev st_mm st_ev ada_acc mod_t mod conv
            cm_mm c_cen c_sq cv_mm c_std c_n2 c_sig c_out vt_mm vt bo gn_mm gn_cen gn_sq gv_mm gn_std
            gn_out mix_mm mix_ss mix_rs mix_rec gtb mul1 x1 rs_2 a2b b2b h2 h2T_tr h2T logits selm negm
            expm gate rk_mm rank2 flag cleared sel_ready gathered xt_ready gu_used glu_ready
            lin_ready sig_done act_tmp act_ready act_tr actT_ready dn_used outp_ready gt_tr gt_ready
            lsum part_up bsel_ready selg_ready combined y_added shifted y_rs fin v_step a_step po_step gtb_ev y_sum gt2b""".split()
        assert len(set(names)) == len(names)
        assert sum(TAPS_U) + Q * (TAPS_K + TAPS_R) + sum(TAPS_BEFORE + LEVELS * n for n in TAPS_BESIDE) >= TAPS * Q
        s = {n: sem(n) for n in names}
        in_win = {kind: sem(f"in_block_{kind}") for kind in win_cols}
        in_ada = list(in_win.values())[0:4]
        in_gu = [sem(f"in_wide_{k}") for k in range(KC)]
        in_ada0 = in_gu
        in_dn = [sem(f"in_dn_{k}") for k in range(KC)]

        from_block = ctx.enter_context(nc.Block())
        block = from_block

        items = [("l1", n, 0, "a") for n in range(3)]
        items += [("w", q, d, "a") for q in range(Q) for d in range(2)]
        items += [("a", q, d, "a") for q in range(Q) for d in range(2)]
        items += [x for q in range(Q) for x in (("cg", q, 0, "a"), ("cv", q, 0, "v"))]
        items += [("k", q, 0, "a") for q in range(Q)]
        items += [("r", q, 0, "v") for q in range(Q)]
        items += [("kn", q, 0, "v") for q in range(Q)]
        items += [("v", g, 0, "v") for g in range(G)]
        FIRST = 5

        def emptied(n, engine):
            return sum(1 for it in items[:n] if it[3] == engine)

        def taken(kind, q):
            n = next(n for n, it in enumerate(items) if it[:2] == (kind, q))
            return emptied(n + 1, items[n][3])

        def bank_of(n):
            return ps[(FIRST + n) % 8]

        def gu_src(e, k):
            return w_gu[bass.ds(e, 1), k * P:(k + 1) * P, :].rearrange("e p n -> p (e n)")

        def dn_src(e, k):
            return w_down[bass.ds(e, 1), k * P:(k + 1) * P, :].rearrange("e p n -> p (e n)")

        @block.sync
        def _(sp):
            sp.dma_start(x0, x_in.rearrange("(g p) d -> p g d", p=P)).then_inc(s["in_x"], 16)
            for k in range(KC):
                sp.dma_start(ada0[:, k, :], ada_w[k * P:(k + 1) * P, 0:2048]).then_inc(in_ada0[k], 16)
            sp.dma_start(lora1, lora1_in).then_inc(s["in_lora"], 16)
            for d in range(2):
                if d == 0:
                    sp.wait_ge(s["pool_zero"], 1)
                sp.dma_start(w2p[64 * d:64 * d + 64, d, :], w2_in[d]).then_inc(s["in_lora"], 16)
                sp.dma_start(a2p[64 * d:64 * d + 64, d, :], a2_in[d]).then_inc(s["in_lora"], 16)
            sp.dma_start(g2, g2_in).then_inc(s["in_lora"], 16)
            for n, (kind, col) in enumerate(win_cols.items()):
                if n == 2:
                    sp.wait_ge(s["ada0_acc"], KC)
                sp.dma_start(win[kind], w_in[:, col:col + CH].rearrange("(k p) n -> p k n", p=P)).then_inc(in_win[kind], 16)
            sp.wait_ge(s["kv_mm"], len(items) - 19)
            sp.dma_start(part_mask, part_in).then_inc(s["in_mod"], 16)
            sp.dma_start(madd, mod_in[0, :, 512:1536].rearrange("p (b n) -> p b n", b=2)).then_inc(s["in_mod"], 16)
            sp.dma_start(mmul, mod_in[1, :, 512:1536].rearrange("p (b n) -> p b n", b=2)).then_inc(s["in_mod"], 16)
            for c in range(16):
                b, k = divmod(c, KC)
                if c >= 4:
                    sp.wait_ge(s["ada_acc"], c - 3)
                if c == 4:
                    sp.dma_start(wout, w_out.rearrange("(k p) n -> p k n", p=P)).then_inc(s["in_wout"], 16)
                sp.dma_start(ada_slot[:, c % 4, :], ada_w[k * P:(k + 1) * P, 2048 * (b + 1):2048 * (b + 2)])\
                    .then_inc(in_ada[c % 4], 16)
            sp.wait_ge(s["st_ev"], 2 * Q)
            for d, out in enumerate((st_f, st_b)):
                sp.dma_start(out.rearrange("(q h) i j -> (h i) q j", h=2), stS[:, d]).then_inc(s["stored"], 16)
            sp.wait_ge(s["ex"], Q)
            sp.dma_start(x1, x_in.rearrange("(g p) d -> p g d", p=P)).then_inc(s["in_x1"], 16)
            sp.wait_ge(s["prep"], Q)
            sp.wait_ge(s["ada_acc"], 16)
            for k in range(4):
                sp.dma_start(wgu[:, k, :], gu_src(0, k)).then_inc(in_gu[k], 16)
            sp.wait_ge(s["st_mm"], Q)
            for k in range(KC):
                sp.dma_start(wdn[:, k, :], dn_src(0, k)).then_inc(in_dn[k], 16)
            sp.wait_ge(s["mix_mm"], 2 * G)
            for k in range(4, KC):
                sp.dma_start(wgu[:, k, :], gu_src(0, k)).then_inc(in_gu[k], 16)

            def load_next(base, e):
                for k in range(KC):
                    sp.wait_ge(s["gu_used"], (base + e) * KC + (k + 1))
                    sp.dma_start(wgu[:, k, :], gu_src(e + 1, k)).then_inc(in_gu[k], 16)
                for k in range(KC):
                    sp.wait_ge(s["dn_used"], (base + e) * KC + (k + 1))
                    sp.dma_start(wdn[:, k, :], dn_src(e + 1, k)).then_inc(in_dn[k], 16)

            with sp.Fori(0, E - 1) as e:
                load_next(0, e)
            sp.wait_ge(s["flag"], 1)
            more = sp.value_load(most_i[0:1, 0:1], min_val=0, max_val=N)
            with sp.If(more > S):
                with sp.Fori(1, N // S) as turn:
                    for k in range(KC):
                        sp.wait_ge(s["gu_used"], turn * (E * KC))
                        sp.dma_start(wgu[:, k, :], gu_src(0, k)).then_inc(in_gu[k], 16)
                    for k in range(KC):
                        sp.wait_ge(s["dn_used"], turn * (E * KC))
                        sp.dma_start(wdn[:, k, :], dn_src(0, k)).then_inc(in_dn[k], 16)
                    with sp.Fori(0, E - 1) as e:
                        load_next(turn * E, e)
            for g, out in enumerate((y_prompt, y_sample)):
                for c in range(2):
                    sp.wait_ge(s["fin"], 2 * g + c + 1)
                    sp.dma_start(out[:, c * 512:(c + 1) * 512], x1[:, g, c * 512:(c + 1) * 512]).then_inc(s["stored"], 16)
            sp.wait_ge(s["stored"], 96)

        def gather(pe, number):
            pe.wait_ge(s["sel_ready"], number)
            for c in range(KC):
                for g in range(G):
                    last = pe.matmul(ps[4 + c // 4][:, (c % 4) * P:(c % 4 + 1) * P], h2[:, g, c * P:(c + 1) * P],
                                     sel[:, g].rearrange("p q s -> p (q s)"), start=(g == 0), stop=(g == G - 1))
                if c % 4 == 3:
                    last.then_inc(s["gathered"], 1)

        def combine(pe, number):
            pe.wait_ge(s["outp_ready"], number * 4)
            for g in range(G):
                for c in range(2):
                    pe.matmul(ps[4 + 2 * g + c], GT[:, g, :], outp[:, c * 512:(c + 1) * 512],
                              start=True, stop=True).then_inc(s["combined"], 1)

        def pe_pair(pe, base, turn, i):
            n = base + i
            for q in range(2):
                arrived = pe.snap(n * 32 + 16 * (q + 2))
                if q == 0:
                    pe.wait_ge(s["xt_ready"], (n + turn) * 2 + 2)
                    pe.wait_ge(s["bsel_ready"], n + turn + 1)
                for r in range(2):
                    for hf in range(2):
                        pe.matmul(ps[r][64 * hf:64 * hf + 64, :], bsel[:, q, :],
                                  bgu[:, r * F + hf * 512:r * F + hf * 512 + 512], start=True, stop=False)
                for k in range(KC):
                    pe.wait_ge(in_gu[k], arrived)
                    for r in range(2):
                        for hf in range(2):
                            last = pe.matmul(ps[r][64 * hf:64 * hf + 64, :], xT[:, k, S * q:S * q + S],
                                             wgu[:, k, r * F + hf * 512:r * F + hf * 512 + 512],
                                             start=False, stop=(k == KC - 1))
                    last.then_inc(s["gu_used"], 1)
                if q == 0:
                    pe.wait_ge(s["gt_ready"], n + 1)
                    combine(pe, n + 1)
                else:
                    pe.wait_ge(s["y_added"], n * 4 + 4)
                    pe.wait_ge(s["selg_ready"], n + 1)
                    for g in range(G):
                        last = pe.transpose(ps[6][:, g * P:(g + 1) * P], selg[:, g].rearrange("p q s -> p (q s)"), ident)
                    last.then_inc(s["gt_tr"], 1)
                    gather(pe, n + turn + 2)
                if q == 1:
                    pe.wait_ge(s["outp_ready"], n * 4 + 6)
                for c in range(2):
                    pe.matmul(ps[2][64 * c:64 * c + 64, :], bsel[:, q, :], bdn[:, c * 512:(c + 1) * 512],
                              start=True, stop=False)
                pe.wait_ge(s["act_ready"], n * 2 + (q + 1))
                pe.wait_ge(s["y_added"], n * 4 + 4)
                for b in range(2):
                    for m in (2 * b, 2 * b + 1):
                        last = pe.transpose(ps[(3, 7)[b]][:, (m % 2) * P:(m % 2 + 1) * P], act[:, m * P:(m + 1) * P], ident)
                    last.then_inc(s["act_tr"], 1)
                for k in range(KC):
                    hf, m = divmod(k, 4)
                    if k in (0, 2):
                        pe.wait_ge(s["actT_ready"], n * 4 + (2 * q + k // 2 + 1))
                    pe.wait_ge(in_dn[k], arrived - 16)
                    for c in range(2):
                        last = pe.matmul(ps[2][64 * c:64 * c + 64, :], actT[:, m, 64 * hf:64 * hf + 64],
                                         wdn[:, k, c * 512:(c + 1) * 512], start=False, stop=(k == KC - 1))
                    last.then_inc(s["dn_used"], 1)

        @block.tensor
        def _(pe):
            pe.wait_ge(s["in_const"], 32)
            pe.wait_ge(s["xn"], 2)
            for c in range(KC):
                for g in range(G):
                    last = pe.transpose(ps[1 + 2 * g + c // 4][:, (c % 4) * T:(c % 4 + 1) * T],
                                        xn[:, g, c * P:(c + 1) * P], ident)
                last.then_inc(s["xT_tr"], 1)
            pe.wait_ge(s["silu"], 1)
            for k in range(KC):
                pe.wait_ge(in_ada0[k], 16)
                for j in range(4):
                    last = pe.matmul(ps[0][32 * j:32 * j + 32, :], siluT[:, k, :], ada0[:, k, j * 512:(j + 1) * 512],
                                     start=(k == 0), stop=(k == KC - 1))
                last.then_inc(s["ada0_acc"], 1)
            pe.wait_ge(s["mod0"], 1)
            for m in range(4):
                last = pe.transpose(ps[5][:, m * P:(m + 1) * P], mod0[:, m * P:(m + 1) * P], ident)
            last.then_inc(s["mod0_tr"], 1)
            for n, (kind, q, d, _e) in enumerate(items):
                out = bank_of(n)
                if n == 0:
                    pe.wait_ge(s["in_lora"], 96)
                    pe.wait_ge(s["hT_a"], KC)
                    pe.wait_ge(s["hT_v"], KC)
                    pe.wait_ge(s["modT"], 1)
                if n >= 8:
                    if items[n - 8][3] == "a":
                        pe.wait_ge(s["a_sig"], emptied(n - 7, "a"))
                    else:
                        pe.wait_ge(s["kk"], emptied(n - 7, "v"))
                if kind == "l1":
                    for k in range(KC):
                        last = pe.matmul(out[:, 0:N], lora1[:, k, q * P:(q + 1) * P], hT[:, k, :],
                                         start=(k == 0), stop=(k == KC - 1))
                elif kind in "wa":
                    pe.wait_ge(s["a_sig"], 3)
                    w2 = w2p if kind == "w" else a2p
                    last = pe.matmul(out[:, 0:N], w2[:, d, q * P:(q + 1) * P], mids[:, "wa".index(kind), :],
                                     start=True, stop=True)
                elif kind == "kn":
                    pe.wait_ge(s["kk_sq"], q + 1)
                    last = pe.matmul(out[:, 0:N], head_ones, sqk[:, q, :], start=True, stop=True)
                elif kind == "v":
                    pe.wait_ge(in_win[kind], 16)
                    for k in range(KC):
                        last = pe.matmul(out, hT[:, k, q * T:(q + 1) * T], win[kind][:, k, :],
                                         start=(k == 0), stop=(k == KC - 1))
                else:
                    pe.wait_ge(in_win[kind], 16)
                    for k in range(KC):
                        last = pe.matmul(out[:, 0:N], win[kind][:, k, q * P:(q + 1) * P], hT[:, k, :],
                                         start=(k == 0), stop=(k == KC - 1))
                last.then_inc(s["kv_mm"] if n >= 19 else s["l2_mm"], 1)

            def ada_part(part):
                b, k0 = part // 2, 4 * (part % 2)
                for k in range(4):
                    pe.wait_ge(in_ada[k], 16 * (part + 2))
                    for j in range(4):
                        last = pe.matmul(ps[3][32 * j:32 * j + 32, :], siluT[:, k0 + k, :],
                                         ada_slot[:, k, j * 512:(j + 1) * 512], start=(k == 0), stop=(k == 3))
                    last.then_inc(s["ada_acc"], 1)

            def norm_mean(r, bank):
                pe.wait_ge(s["o_ev"], 2 * r + 2)
                pe.matmul(ps[5][:, 0:N], head_ones, oT[:, r, :], start=True, stop=True).then_inc(s["gn_mm"], 1)
                pe.matmul(bank[:, 0:N], g2[:, r * P:(r + 1) * P], mids[:, 2, :], start=True, stop=True)
                for g in range(G):
                    last = pe.transpose(bank[:, N + g * T:N + (g + 1) * T], V[:, g, r * P:(r + 1) * P], ident)
                last.then_inc(s["vt_mm"], 1)

            def norm_var(r):
                pe.wait_ge(s["gn_sq"], r + 1)
                pe.wait_ge(s["rsum"], 3 * r + 3)
                pe.matmul(ps[7][:, 0:N], head_ones, sq[:, r, :], start=True, stop=True)
                pe.matmul(ps[7][:, N:2 * N], head_ones, rkk[:, r, :], start=True, stop=True).then_inc(s["gv_mm"], 1)

            def conv_sum(src, signal):
                for q in range(Q):
                    last = pe.matmul(ps[6][:, 0:A_COLS], ones, src[:, q, :], start=(q == 0), stop=(q == Q - 1))
                last.then_inc(s[signal], 1)

            for q in range(Q):
                w = q % 2
                pe.wait_ge(s["prep"], q + 1)
                pe.wait_ge(s["prep_s"], q + 1)
                if q == 0:
                    pe.wait_ge(s["a_sig"], emptied(len(items), "a"))
                    pe.wait_ge(s["kk"], emptied(len(items), "v"))
                for g in range(G):
                    for i in range(4):
                        h, d = divmod(i, 2)
                        n = 8 * q + 4 * g + i
                        if n >= 2:
                            pe.wait_ge(s["m_ev"], n - 1)
                        if i < 2 and g == 0 and q > 0:
                            pe.wait_ge(s["sa_ev"], 2 * q)
                        for k in range(2):
                            last = pe.matmul(ps[6 + n % 2][:, 256 * k:256 * k + 256], kbp[:, g, k, h, d, :],
                                             ra[:, w, g, d].rearrange("p k t -> p (k t)"), start=True, stop=True)
                        last.then_inc(s["m_mm"], 1)
                if q > 0:
                    norm_mean(q - 1, ps[0])
                if q > 0:
                    pe.wait_ge(s["x_up"], 12 * q)
                for k in range(2):
                    for d in range(2):
                        for h in range(2):
                            last = pe.matmul(ps[4][:, (2 * k + d) * P:(2 * k + d + 1) * P], kbp[:, 0, k, h, d, :],
                                             dgm[:, w, d, :], start=(h == 0), stop=(h == 1))
                last.then_inc(s["bt_mm"], 1)
                pe.wait_ge(s["m_ev"], 8 * q + 8)
                for g in range(G):
                    if g == 0 and q > 0:
                        pe.wait_ge(s["st_ev"], 2 * q)
                    if g == 1:
                        pe.wait_ge(s["bt_ev"], q + 1)
                    pe.wait_ge(s["lsum"], 2 * q + g + 1)
                    for h in range(2):
                        last = pe.matmul(ps[2 + 2 * g][:, h * P:(h + 1) * P], LT[:, g, h, 0, 3, :], ident,
                                         start=True, stop=True)
                    last.then_inc(s["d_mm"], 1)
                for g in range(G):
                    if g == 1:
                        for d in range(2):
                            pe.matmul(ps[7][:, d * P:(d + 1) * P], ra[:, w, 1, d, 1, :], S0s[:, w, d, :],
                                      start=(d == 0), stop=False, skip_group_check=True)
                    for i in range(4):
                        h, d = divmod(i, 2)
                        last = pe.matmul(ps[6 + g][:, d * P + h * HD:d * P + h * HD + HD], LT[:, g, h, d, 1, :],
                                         V[:, g, q * P + h * HD:q * P + h * HD + HD],
                                         start=(g == 0), stop=True, skip_group_check=True)
                    last.then_inc(s["w_mm"], 1)
                for lv in range(1, LEVELS):
                    for g in range(G):
                        pe.wait_ge(s["x_up"], 12 * q + 2 * (lv - 1) + g + 1)
                        if lv == 1 and q > 0:
                            pe.wait_ge(s["o_ev"], 2 * (q - 1) + g + 1)
                            pe.wait_ge(s["vt"], q)
                        for h in range(2):
                            last = pe.matmul(ps[g][:, h * P:(h + 1) * P], LT[:, g, h, 0, 3, :], X[:, g, 1, h, :],
                                             start=True, stop=True)
                        last.then_inc(s["p_mm"], 1)
                    if lv == 1 and q > 0:
                        pe.wait_ge(s["w_ev"], 2 * q + 2)
                        norm_var(q - 1)
                    if lv == 2 and q == Q - 1:
                        pe.wait_ge(s["conv"], TAPS * Q)
                        conv_sum(acc, "cm_mm")
                    if lv == 4 and q == Q - 1:
                        pe.wait_ge(s["c_sq"], 1)
                        conv_sum(csq, "cv_mm")
                    for g in range(G):
                        pe.wait_ge(s["p_ev"], 12 * q + 2 * (lv - 1) + g + 1)
                        pe.wait_ge(s["y_up"], 14 * q + 2 * (lv - 1) + g + 1)
                        part = 1 + lv % 2
                        if lv == 1 and g == 0 and q > 0:
                            pe.wait_ge(s["mod_t"], q)
                        if lv < LEVELS - 1:
                            for h in range(2):
                                last = pe.matmul(ps[2 + 2 * g][:, h * P:(h + 1) * P], Y[:, g, part, h, :],
                                                 Pn[:, g, h, :], start=True, stop=True)
                            last.then_inc(s["d_mm"], 1)
                        for h in range(2):
                            last = pe.matmul(ps[3 + 2 * g][:, h * P:(h + 1) * P], Pn[:, g, h, :],
                                             Y[:, g, part, h, :], start=True, stop=True)
                        last.then_inc(s["e_mm"], 1)
                for g in range(G):
                    pe.wait_ge(s["y_up"], 14 * q + 12 + g + 1)
                    pe.wait_ge(s["w_ev"], 2 * q + g + 1)
                    if g == 1 and q > 0:
                        pe.wait_ge(s["bo"], q)
                    if g == 0 and q == Q - 1:
                        pe.wait_ge(s["c_std"], 1)
                    for i in range(4):
                        h, d = divmod(i, 2)
                        c = d * P + h * HD
                        last = pe.matmul(ps[6 + g][:, 256 + c:256 + c + HD], X[:, g, d, h, :],
                                         W[:, g, d, h * HD:h * HD + HD], start=True, stop=True)
                    last.then_inc(s["sa_mm"], 1)
                ada_part(q)
                for g in range(G):
                    if g == 1:
                        for d in range(2):
                            pe.matmul(ps[1][:, 0:T], S0s[:, w, d, :], ra[:, w, 1, d, 0, :], start=(d == 0),
                                      stop=False, skip_group_check=True)
                    for i in range(4):
                        h, d = divmod(i, 2)
                        pe.matmul(ps[g][HD * h:HD * h + HD, 0:T], V[:, g, q * P + h * HD:q * P + h * HD + HD],
                                  LT[:, g, h, d, 0, :], start=(g == 0 and d == 0), stop=False, skip_group_check=True)
                    pe.wait_ge(s["sa_ev"], 2 * q + g + 1)
                    for i in range(4):
                        h, d = divmod(i, 2)
                        last = pe.matmul(ps[g][HD * h:HD * h + HD, 0:T], SA[:, g, d, h * HD:h * HD + HD],
                                         LT[:, g, h, d, 2, :], start=False, stop=(d == 1), skip_group_check=True)
                    last.then_inc(s["y_mm"], 1)
                for d in range(2):
                    pe.matmul(ps[2][:, d * P:(d + 1) * P], SA[:, 0, d, :], bkT[:, 1, d, :], start=True, stop=False)
                    last = pe.matmul(ps[2][:, d * P:(d + 1) * P], V[:, 0, q * P:(q + 1) * P], bkT[:, 0, d, :],
                                     start=False, stop=True)
                last.then_inc(s["st_mm"], 1)

            def spread(b, j0, banks, groups=range(G)):
                for g in groups:
                    for c in range(2):
                        row = 32 * (j0 + c) + g
                        last = pe.matmul(ps[banks + 2 * g + c], ident[:, row:row + 1].broadcast_to([P, P]), mod[:, b, :],
                                         start=True, stop=True)
                return last

            def spread_to(b, j0, g, banks):
                for c in range(2):
                    row = 32 * (j0 + c) + g
                    last = pe.matmul(ps[banks[c]], ident[:, row:row + 1].broadcast_to([P, P]), mod[:, b, :],
                                     start=True, stop=True)
                return last

            norm_mean(Q - 1, ps[4])

            def project(k):
                for n in range(4):
                    g, c = divmod(n, 2)
                    lhs = cvT[:, k, g * T:(g + 1) * T] if k < Q else oT[:, k - Q, g * T:(g + 1) * T]
                    last = pe.matmul(ps[n], lhs, wout[:, k, c * 512:(c + 1) * 512], start=(k == 0), stop=(k == KC - 1))
                    if k == KC - 1:
                        last.then_inc(s["mix_mm"], 1)

            pe.wait_ge(s["in_wout"], 16)
            pe.wait_ge(s["st_ev"], 2 * Q)
            pe.wait_ge(s["mod_t"], Q)
            for k in range(Q):
                pe.wait_ge(s["c_out"], k + 1)
                project(k)
                if k == 0:
                    norm_var(Q - 1)
            pe.wait_ge(s["gn_out"], Q - 1)
            for k in range(Q, KC - 1):
                project(k)
            pe.wait_ge(s["mod"], 2)
            pe.wait_ge(s["vt"], Q)
            pe.wait_ge(s["bo"], Q)
            spread(0, 0, 4).then_inc(s["gtb"], 1)
            pe.wait_ge(s["gn_out"], Q)
            project(KC - 1)
            pe.wait_ge(s["gtb_ev"], 4)
            spread(1, 0, 4).then_inc(s["a2b"], 1)
            for g in range(G):
                pe.wait_ge(s["mul1"], 2 * g + 2)
                spread(0, 2, 0, (g,)).then_inc(s["b2b"], 1)
            for g in range(G):
                pe.wait_ge(s["h2"], 2 * g + 2)
                for c in range(KC):
                    last = pe.transpose(ps[4 + 2 * g + c // 4][:, (c % 4) * P:(c % 4 + 1) * P],
                                        h2[:, g, c * P:(c + 1) * P], ident)
                    if c % 4 == 3:
                        last.then_inc(s["h2T_tr"], 1)
            pe.wait_ge(s["in_router"], 16 * 4)
            for g in range(G):
                pe.wait_ge(s["h2T"], 2 * g + 2)
                for c in range(KC):
                    last = pe.matmul(ps[g][:, 0:E], h2T[:, c, g * T:(g + 1) * T], rw[:, c, :],
                                     start=(c == 0), stop=(c == KC - 1))
                last.then_inc(s["logits"], 1)
            pe.wait_ge(s["selm"], 2)
            pe.matmul(ps[2][:, 0:E], upper, sel_m[:, 0, :], start=True, stop=True)
            pe.matmul(ps[2][:, E:2 * E], upper, sel_m[:, 1, :], start=True, stop=False)
            pe.matmul(ps[2][:, E:2 * E], ones, sel_m[:, 0, :], start=False, stop=True)
            for g in range(G):
                last = pe.matmul(ps[2][:, 2 * E:3 * E], ones, sel_m[:, g, :], start=(g == 0), stop=(g == 1))
            last.then_inc(s["rk_mm"], 1)
            gather(pe, 1)
            with pe.Fori(0, E // 2) as i:
                pe_pair(pe, 0, 0, i)
            pe.wait_ge(s["flag"], 1)
            more = pe.value_load(most_i[0:1, 0:1], min_val=0, max_val=N)
            with pe.If(more > S):
                with pe.Fori(1, N // S) as turn:
                    gather(pe, turn * (E // 2 + 1) + 1)
                    with pe.Fori(0, E // 2) as i:
                        pe_pair(pe, turn * (E // 2), turn, i)
                spread_to(1, 2, 0, (0, 1)).then_inc(s["gt2b"], 1)
                pe.wait_ge(s["gt_ready"], (N // S) * (E // 2) + 1)
                combine(pe, (N // S) * (E // 2) + 1)
            with pe.Else():
                spread_to(1, 2, 0, (0, 1)).then_inc(s["gt2b"], 1)
                pe.wait_ge(s["gt_ready"], E // 2 + 1)
                combine(pe, E // 2 + 1)
            spread_to(1, 2, 1, (2, 3)).then_inc(s["gt2b"], 1)

        def take_gathered(a, number):
            for b in range(2):
                a.wait_ge(s["gathered"], number * 2 - 1 + b)
                a.activation(xT[:, 4 * b:4 * b + 4, :].rearrange("p c s -> p (c s)"), ps[4 + b], ACT.Copy)\
                    .then_inc(s["xt_ready"], 1)

        def act_pair(a, base, turn, i):
            n = base + i
            for q in range(2):
                a.wait_ge(s["glu_ready"], n * 2 + (q + 1))
                a.activation(sig, glu, ACT.Sigmoid, scale=1.702).then_inc(s["sig_done"], 1)
                if q == 1:
                    a.wait_ge(s["gt_tr"], n + 1)
                    a.activation(GT.rearrange("p g t -> p (g t)"), ps[6][:, 0:N], ACT.Copy).then_inc(s["gt_ready"], 1)
                    take_gathered(a, n + turn + 2)
                for b in range(2):
                    a.wait_ge(s["act_tr"], n * 4 + (2 * q + b + 1))
                    a.activation(actT[:, 2 * b:2 * b + 2, :].rearrange("p m t -> p (m t)"), ps[(3, 7)[b]][:, 0:256],
                                 ACT.Copy).then_inc(s["actT_ready"], 1)
                a.wait_ge(s["dn_used"], n * 16 + KC * (q + 1))
                a.activation(outp[64 * q:64 * q + 64, 512:1024], ps[2][64:128, :], ACT.Copy).then_inc(s["outp_ready"], 1)

        @block.scalar
        def _(a):
            a_at = Steps()
            a.dma_start(const, const_in).then_inc(s["in_const"], 16)
            a.wait_ge(s["silu_pad"], 1)
            a.dma_start(siluT[:, :, 0:G], cond_in).then_inc(s["in_cond"], 16)
            a.dma_start(chan, chan_in).then_inc(s["in_const"], 16)
            a.dma_start(madd0, mod_in[0, :, 0:512]).then_inc(s["in_mod"], 16)
            a.dma_start(mmul0, mod_in[1, :, 0:512]).then_inc(s["in_mod"], 16)
            a.dma_start(level_f, level_in).then_inc(s["in_rw"], 16)
            a.wait_ge(s["in_x"], 16)
            for g in range(G):
                a.activation(junk0, x0[:, g, :], ACT.Square, accum_out=ssx[:, g:g + 1]).then_inc(s["a_step"], a_at.mark("ms_x"))
                a.wait_ge(s["a_step"], a_at.after("ms_x", g + 1))
            a.wait_ge(s["in_const"], 32)
            a.activation(rsx[:, 0:G], ssx[:, 0:G], ACT.Sqrt, scale=1.0 / D, bias=eps[0]).then_inc(s["rs_x"], 1)
            a.wait_ge(s["in_cond"], 16)
            a.activation(junk0[:, 0:KC * 32], siluT.rearrange("p k m -> p (k m)"), ACT.Sigmoid).then_inc(s["silu_sig"], 1)
            a.wait_ge(s["xT_tr"], KC)
            a.wait_ge(s["modT"], 1)
            for c in range(KC):
                hf, m = divmod(c, 4)
                a.activation(hT[:, c, 0:T], ps[1 + c // 4][:, (c % 4) * T:(c % 4 + 1) * T], ACT.Identity,
                             scale=modT[:, m, 32 * (2 + hf):32 * (2 + hf) + 1],
                             bias=modT[:, m, 32 * hf:32 * hf + 1]).then_inc(s["hT_a"], 1)
            def decays(r):
                a.wait_ge(s["pre"], 8 * G)
                if r > 0:
                    a.wait_ge(s["prep"], r)
                    a.wait_ge(s["prep_s"], r)
                for sg, sc in enumerate((-KAPPA, KAPPA)):
                    last = a.activation(Ex[:, sg], Pc[:, :, r], ACT.Exp, scale=sc)
                last.then_inc(s["ex"], 1)

            for n, (kind, q, d, e) in enumerate(items):
                if e != "a":
                    continue
                out = bank_of(n)
                if n >= 19:
                    a.wait_ge(s["kv_mm"], n - 18)
                else:
                    a.wait_ge(s["l2_mm"], n + 1)
                if kind == "l1":
                    ins = a.activation(mids[:, q, :], out[:, 0:N], (ACT.Tanh, ACT.Copy, ACT.Sigmoid)[q])
                elif kind == "w":
                    ins = a.activation(sgw[:, 2 * q + d, :], out[:, 0:N], ACT.Sigmoid, bias=chan[:, q, C_W0 + d:C_W0 + d + 1])
                elif kind == "a":
                    ins = a.activation(aT[:, d, q, :], out[:, 0:N], ACT.Sigmoid, bias=chan[:, q, C_A0 + d:C_A0 + d + 1])
                elif kind == "k":
                    if q == 0:
                        a.wait_ge(s["level"], 1)
                    ins = a.activation(kT[:, q, :], out[:, 0:N], ACT.Copy)
                elif kind == "cg":
                    ins = a.activation(sgc[:, q, :], out[:, 0:N], ACT.Sigmoid)
                ins.then_inc(s["a_sig"], 1)
                if kind == "k":
                    a.wait_ge(s["a_sig"], emptied(n + 1, "a"))
                    a.wait_ge(s["kk_raw"], q + 1)
                    a.activation(sqk[:, q, :], kkT[:, q, :], ACT.Square).then_inc(s["kk_sq"], 1)
                if kind == "k" and q == Q - 1:
                    a.wait_ge(s["kk"], taken("kn", Q - 1))
                    a.activation(rn.rearrange("p q t -> p (q t)"), rn.rearrange("p q t -> p (q t)"), ACT.Sqrt)\
                        .then_inc(s["kk_sqrt"], 1)
                    decays(0)
            def norm_copy(r, bank):
                a.wait_ge(s["vt_mm"], r + 1)
                a.activation(gT[:, r, :], bank[:, 0:N], ACT.Copy)
                a.activation(vT[:, r, :], bank[:, N:2 * N], ACT.Copy).then_inc(s["vt"], 1)
                a.wait_ge(s["gn_cen"], r + 1)
                a.activation(sq[:, r, :], oc[:, r, :], ACT.Square).then_inc(s["gn_sq"], 1)

            def norm_std(r):
                a.wait_ge(s["gv_mm"], r + 1)
                a.activation(sq[:, r, :], ps[7][:, 0:N], ACT.Sqrt, scale=1.0 / HD, bias=eps[2]).then_inc(s["gn_std"], 1)

            for q in range(Q):
                if q > 0:
                    norm_copy(q - 1, ps[0])
                a.wait_ge(s["bt_mm"], q + 1)
                a.activation(r_bk, ps[4], ACT.Copy).then_inc(s["bt_ev"], 1)
                for g in range(G):
                    a.wait_ge(s["w_mm"], 2 * q + g + 1)
                    a.activation(W[:, g].rearrange("p d i -> p (d i)"), ps[6 + g][:, 0:256], ACT.Copy)\
                        .then_inc(s["w_ev"], 1)
                for lv in range(1, LEVELS):
                    for g in range(G):
                        n = 12 * q + 2 * (lv - 1) + g + 1
                        a.wait_ge(s["p_mm"], n)
                        if n > 2:
                            a.wait_ge(s["e_mm"], n - 2)
                        a.activation(Pn[:, g].rearrange("p h t -> p (h t)"), ps[g][:, 0:2 * P], ACT.Copy).then_inc(s["p_ev"], 1)
                    if lv == 1 and q > 0:
                        norm_std(q - 1)
                    if lv == 2 and q < Q - 1:
                        decays(q + 1)
                    if lv == 3 and q == Q - 1:
                        a.wait_ge(s["c_cen"], Q)
                        a.activation(csq.rearrange("p q t -> p (q t)"), acc.rearrange("p q t -> p (q t)"), ACT.Square)\
                            .then_inc(s["c_sq"], 1)
                    if lv == 4 and q == Q - 1:
                        a.wait_ge(s["cv_mm"], 1)
                        a.activation(crs, ps[6][:, 0:A_COLS], ACT.Sqrt, scale=1.0 / CH, bias=eps[1]).then_inc(s["c_std"], 1)
                    if lv == 6 and q == Q - 1:
                        a.wait_ge(s["c_n2"], Q)
                        a.activation(csg.rearrange("p q t -> p (q t)"), acc.rearrange("p q t -> p (q t)"), ACT.Sigmoid)\
                            .then_inc(s["c_sig"], 1)
                for g in range(G):
                    a.wait_ge(s["sa_mm"], 2 * q + g + 1)
                    a.activation(SA[:, g].rearrange("p d i -> p (d i)"), ps[6 + g][:, 256:512], ACT.Copy)\
                        .then_inc(s["sa_ev"], 1)
                for g in range(G):
                    a.wait_ge(s["y_mm"], 2 * q + g + 1)
                    a.activation(oT[:, q, g * T:(g + 1) * T], ps[g][:, 0:T], ACT.Copy).then_inc(s["o_ev"], 1)
                a.wait_ge(s["st_mm"], q + 1)
                for h in range(2):
                    a.activation(stS[HD * h:HD * h + HD, :, q, :],
                                 ps[2][HD * h:HD * h + HD, 0:256].rearrange("p (d j) -> p d j", d=2)[:, :, HD * h:HD * h + HD],
                                 ACT.Copy).then_inc(s["st_ev"], 1)
            norm_copy(Q - 1, ps[4])
            norm_std(Q - 1)
            a.wait_ge(s["gtb"], 1)
            for n in range(4):
                a.activation(gtb[:, n, :], ps[4 + n], ACT.Copy).then_inc(s["gtb_ev"], 1)
            for g in range(G):
                for n in (2 * g, 2 * g + 1):
                    a.wait_ge(s["mix_mm"], n + 1)
                    a.activation(junk[:, 512 * (n % 2):512 * (n % 2) + 512], ps[n], ACT.Square, accum_out=ssm[:, n:n + 1])\
                        .then_inc(s["mix_ss"], 1)
                a.wait_ge(s["mix_rs"], g + 1)
                a.activation(rsm[:, g:g + 1], rsm[:, g:g + 1], ACT.Sqrt, scale=1.0 / D, bias=eps[0]).then_inc(s["mix_rec"], 1)
            for g in range(G):
                a.wait_ge(s["x1"], 2 * g + 2)
                a.activation(junk, x1[:, g, :], ACT.Square, accum_out=ss2[:, g:g + 1]).then_inc(s["a_step"], a_at.mark("ms_2"))
                a.wait_ge(s["a_step"], a_at.after("ms_2", g + 1))
                a.activation(rs2[:, g:g + 1], ss2[:, g:g + 1], ACT.Sqrt, scale=1.0 / D, bias=eps[0]).then_inc(s["rs_2"], 1)
            for n in range(4):
                g, b = divmod(n, 2)
                a.wait_ge(s["h2T_tr"], n + 1)
                a.activation(h2T[:, 4 * b:4 * b + 4, g * T:(g + 1) * T], ps[4 + n].rearrange("p (c t) -> p c t", c=4), ACT.Copy)\
                    .then_inc(s["h2T"], 1)
            for g in range(G):
                a.wait_ge(s["negm"], g + 1)
                a.activation(ex[:, g, :], ext[:, g, 0:E], ACT.Exp, bias=negm[:, g:g + 1]).then_inc(s["expm"], 1)
            take_gathered(a, 1)
            with a.Fori(0, E // 2) as i:
                act_pair(a, 0, 0, i)
            a.wait_ge(s["flag"], 1)
            more = a.value_load(most_i[0:1, 0:1], min_val=0, max_val=N)
            with a.If(more > S):
                with a.Fori(1, N // S) as turn:
                    take_gathered(a, turn * (E // 2 + 1) + 1)
                    with a.Fori(0, E // 2) as i:
                        act_pair(a, turn * (E // 2), turn, i)
            a.activation(ss2[:, 0:1], rs2[:, 0:1], ACT.Sqrt)
            for g in range(G):
                a.wait_ge(s["y_sum"], 2 * g + 2)
                a.activation(junk, yacc[:, g, :], ACT.Square, accum_out=ssm[:, g:g + 1]).then_inc(s["a_step"], a_at.mark("y_ss"))
                a.wait_ge(s["a_step"], a_at.after("y_ss", g + 1))
                a.activation(rsm[:, g:g + 1], ssm[:, g:g + 1], ACT.Sqrt, scale=1.0 / D, bias=eps[0]).then_inc(s["y_rs"], 1)

        @block.gpsimd
        def _(po):
            po_at = Steps()
            po.memset(siluT, 0.0).then_inc(s["silu_pad"], 1)
            po.memset(r_L[:, 3072:5120], 0.0).then_inc(s["pool_zero"], 1)
            po.memset(r_u, 0.0)
            po.memset(S0.rearrange("p w d j -> p (w d j)"), 0.0).then_inc(s["pool_zero"], 1)
            po.wait_ge(s["pool_zero"], 2)
            for r in range(2):
                for h in range(2):
                    po.dma_start(S0[HD * h:HD * h + HD, r, :, HD * h:HD * h + HD],
                                 s0_in[:, 2 * r + h].rearrange("d j i -> j d i")).then_inc(s["s0_in"], 16)
            po.wait_ge(s["in_rw"], 16)
            po.tensor_copy(level[:, :, :, :], level_f).then_inc(s["level"], 1)
            po.wait_ge(s["l2_mm"], 19)
            po.wait_ge(s["level"], 1)
            for h in range(2):
                other = 1 - h
                last = po.memset(kbp[HD * other:HD * other + HD, :, :, h], 0.0)
            last.then_inc(s["pool_zero"], 1)
            po.wait_ge(s["in_const"], 32)
            po.wait_ge(s["pool_zero"], 3)
            po.tensor_scalar(omka, chan[:, :, C_KA], -1.0, 1.0, ALU.mult, ALU.add).then_inc(s["po_step"], po_at.mark("omka"))
            po.wait_ge(s["po_step"], po_at.after("omka", 1))
            def scaled_keys(q):
                if q == 0:
                    po.wait_ge(s["a_sig"], taken("k", Q - 1))
                po.wait_ge(s["kk_mm"], q + 1)
                if q > 0:
                    po.wait_ge(s["prep"], q)
                    po.wait_ge(s["rsum"], 3 * q)
                po.tensor_scalar(kd, aT[:, :, q, :], chan[:, q, C_KA:C_KA + 1], omka[:, q:q + 1], ALU.mult, ALU.add)\
                    .then_inc(s["po_step"], po_at.mark("scaled"))
                po.wait_ge(s["po_step"], po_at.after("scaled", q + 1))
                po.tensor_tensor(kd, kd, kT[:, q, :].unsqueeze(1).broadcast_to([P, 2, N]), ALU.mult)
                po.tensor_tensor(bv, aT[:, :, q, :], kkT[:, q, :].unsqueeze(1).broadcast_to([P, 2, N]), ALU.mult)\
                    .then_inc(s["kdb"], 1)

            def scaled_states(q):
                w = q % 2
                po.wait_ge(s["ex"], q + 1)
                po.wait_ge(s["s0_in"], 64 if q < 2 else 128)
                if q >= 2:
                    po.wait_ge(s["st_mm"], q - 1)
                for d in range(2):
                    po.tensor_scalar(dgm[:, w, d, :], ident, Ex[:, 0, d, 0, T:T + 1], None, ALU.mult)
                    last = po.tensor_scalar(S0s[:, w, d, :], S0[:, w, d, :], Ex[:, 0, d, 1, T:T + 1], None, ALU.mult)
                last.then_inc(s["prep_s"], 1)
                if q < 2:
                    po.wait_ge(s["prep_s"], q + 1)
                    for h in range(2):
                        po.dma_start(S0[HD * h:HD * h + HD, w, :, HD * h:HD * h + HD],
                                     s0_in[:, 2 * (q + 2) + h].rearrange("d j i -> j d i")).then_inc(s["s0_in"], 16)

            scaled_keys(0)
            scaled_states(0)
            for q in range(Q):
                if q > 0:
                    po.wait_ge(s["sa_mm"], 2 * q)
                else:
                    po.wait_ge(s["kv_mm"], len(items) - 19)
                four = ident.unsqueeze(1).broadcast_to([P, 4, P])
                two = ident.unsqueeze(1).broadcast_to([P, 2, P])
                for g in range(G):
                    po.tensor_copy(X[:, g].rearrange("p c h t -> p (c h) t"), four)
                    po.tensor_copy(Y[:, g, 0], two)
                    po.tensor_copy(Y[:, g, 2], two).then_inc(s["xy"], 1)
                po.wait_ge(s["kdb"], q + 1)
                po.tensor_tensor(rkk[:, q, :], kd[:, 0, :], kd[:, 1, :], ALU.add).then_inc(s["rsum"], 1)
                po.wait_ge(s["rsum"], 3 * q + 1)
                po.tensor_tensor(rkk[:, q, :], rkk[:, q, :], rT[:, q, :], ALU.mult).then_inc(s["rsum"], 1)
                po.wait_ge(s["rsum"], 3 * q + 2)
                po.tensor_scalar(rkk[:, q, :], rkk[:, q, :], chan[:, q, C_RK:C_RK + 1], None, ALU.mult)\
                    .then_inc(s["rsum"], 1)
                if q == 0:
                    po.wait_ge(s["in_mod"], 80)
                for lv in range(1, LEVELS):
                    for g in range(G):
                        n = 6 * 2 * q + 2 * (lv - 1) + g + 1
                        if lv < LEVELS - 1:
                            part = part_mask[:, lv - 1, :].unsqueeze(1).broadcast_to([P, 2, T])
                            po.wait_ge(s["x_up"], n)
                            po.wait_ge(s["p_mm"], n)
                            po.tensor_tensor(X[:, g, 1], X[:, g, 0], part, ALU.mult).then_inc(s["part_up"], 1)
                            po.wait_ge(s["y_up"], 7 * 2 * q + 2 * (lv - 1) + g + 1)
                            po.tensor_tensor(Y[:, g, 1 + (lv + 1) % 2], Y[:, g, 0], part, ALU.mult).then_inc(s["part_up"], 1)
                        else:
                            po.wait_ge(s["y_up"], 7 * 2 * q + 2 * (lv - 1) + g + 1)
                            po.wait_ge(s["p_mm"], n)
                            for d in range(2):
                                last = po.tensor_tensor(X[:, g, d], Y[:, g, 0], mask_lt[:, d, 0, :].unsqueeze(1).broadcast_to([P, 2, T]),
                                                        ALU.mult)
                            last.then_inc(s["part_up"], 1)
                if q < Q - 1:
                    scaled_keys(q + 1)
                    scaled_states(q + 1)
            po.wait_ge(s["prep"], Q)
            po.wait_ge(s["prep_s"], Q)
            po.dma_start(rw, router_w.rearrange("(k p) e -> p k e", p=P)).then_inc(s["in_router"], 16)
            po.dma_start(rb, router_b.partition_broadcast(P)).then_inc(s["in_router"], 16)
            po.dma_start(bdn, b_down).then_inc(s["in_router"], 16)
            po.wait_ge(s["y_mm"], 2 * Q)
            po.dma_start(bgu, b_gu).then_inc(s["in_router"], 16)

        def choose(v, i):
            for q in range(2):
                for g in range(G):
                    last = v.tensor_scalar(sel[:, g, q, :], iota, rank[:, g, bass.ds(i * 2 + q, 1)], None, ALU.is_equal)
            last.then_inc(s["sel_ready"], 1)

        def choose_bias(v, i):
            for q in range(2):
                last = v.tensor_copy(bsel[:, q, :], ident[0:E, bass.ds(i * 2 + q, 1)].broadcast_to([E, S]))
            last.then_inc(s["bsel_ready"], 1)

        def add_outputs(v, number, signal="y_added"):
            for g in range(G):
                for c in range(2):
                    v.wait_ge(s["combined"], number * 4 - 3 + (2 * g + c))
                    v.tensor_tensor(yacc[:, g, c * 512:(c + 1) * 512], yacc[:, g, c * 512:(c + 1) * 512],
                                    ps[4 + 2 * g + c], ALU.add).then_inc(s[signal], 1)

        def dve_pair(v, base, turn, i):
            n = base + i
            for q in range(2):
                v.wait_ge(s["gu_used"], n * 16 + KC * (q + 1))
                v.tensor_scalar(glu, ps[0], 7.0, None, ALU.min).then_inc(s["glu_ready"], 1)
                v.tensor_scalar(lin, ps[1], 7.0, -7.0, ALU.min, ALU.max).then_inc(s["lin_ready"], 1)
                v.wait_ge(s["lin_ready"], n * 2 + (q + 1))
                v.scalar_tensor_tensor(lin, lin, 1.0, glu, ALU.add, ALU.mult).then_inc(s["act_tmp"], 1)
                v.wait_ge(s["act_tmp"], n * 2 + (q + 1))
                v.wait_ge(s["sig_done"], n * 2 + (q + 1))
                v.tensor_tensor(act, lin, sig, ALU.mult).then_inc(s["act_ready"], 1)
                if q == 0:
                    add_outputs(v, n + 1)
                    for qq in range(2):
                        for g in range(G):
                            last = v.tensor_scalar(selg[:, g, qq, :], iota, rank[:, g, bass.ds(i * 2 + qq, 1)],
                                                   gate[:, g, bass.ds(i * 2 + qq, 1)], ALU.is_equal, ALU.mult)
                    last.then_inc(s["selg_ready"], 1)
                    choose(v, i + 1)
                else:
                    v.wait_ge(s["dn_used"], n * 16 + KC + 1)
                    choose_bias(v, i + 1)
                v.wait_ge(s["dn_used"], n * 16 + KC * (q + 1))
                v.tensor_copy(outp[64 * q:64 * q + 64, 0:512], ps[2][0:64, :]).then_inc(s["outp_ready"], 1)

        @block.vector
        def _(v):
            v_at = Steps()
            v.wait_ge(s["rs_x"], 1)
            v.reciprocal(rsx[:, 0:G], rsx[:, 0:G]).then_inc(s["rs_x"], 1)
            v.wait_ge(s["rs_x"], 2)
            for g in range(G):
                v.tensor_scalar(xn[:, g, :], x0[:, g, :], rsx[:, g:g + 1], None, ALU.mult).then_inc(s["xn"], 1)
            v.wait_ge(s["silu_sig"], 1)
            v.tensor_tensor(siluT.rearrange("p k m -> p (k m)"), siluT.rearrange("p k m -> p (k m)"),
                            junk0[:, 0:KC * 32], ALU.mult).then_inc(s["silu"], 1)
            v.wait_ge(s["in_mod"], 32)
            v.wait_ge(s["ada0_acc"], KC)
            v.tensor_tensor(mod0, ps[0], madd0, ALU.add).then_inc(s["v_step"], v_at.mark("mod0_t"))
            v.wait_ge(s["v_step"], v_at.after("mod0_t", 1))
            v.scalar_tensor_tensor(mod0, mod0, const[:, K_ONE:K_ONE + 1], mmul0, ALU.add, ALU.mult).then_inc(s["mod0"], 1)
            v.wait_ge(s["mod0_tr"], 1)
            v.tensor_copy(modT.rearrange("p m r -> p (m r)"), ps[5]).then_inc(s["modT"], 1)
            v.wait_ge(s["modT"], 1)
            v.wait_ge(s["xT_tr"], KC)
            for c in range(KC):
                hf, m = divmod(c, 4)
                v.tensor_scalar(hT[:, c, T:N], ps[3 + c // 4][:, (c % 4) * T:(c % 4 + 1) * T],
                                modT[:, m, 32 * (2 + hf) + 1:32 * (2 + hf) + 2], modT[:, m, 32 * hf + 1:32 * hf + 2],
                                ALU.mult, ALU.add).then_inc(s["hT_v"], 1)
            for q in range(Q):
                for d in range(2):
                    n = 2 * q + d
                    v.wait_ge(s["a_sig"], 4 + n)
                    for g in range(G):
                        run = Pc[:, d, q, g, :]
                        v.memset(run[:, 0:1], 0.0)
                        v.tensor_tensor_scan(run[:, 1:T + 1], ones, sgw[:, n, g * T:(g + 1) * T], 0.0,
                                             ALU.mult, ALU.add).then_inc(s["scan"], 1)
                for d in range(2):
                    for g in range(G):
                        n = 4 * q + 2 * d + g
                        half = ssx[:, 0:1] if n % 2 == 0 else ssx[:, 1:2]
                        run = Pc[:, d, q, g, :]
                        v.wait_ge(s["scan"], n + 1)
                        if n >= 2:
                            v.wait_ge(s["pre"], n - 1)
                        v.tensor_scalar(half, run[:, T:T + 1], 0.5, None, ALU.mult).then_inc(s["v_step"], v_at.mark("sgw_used"))
                        v.wait_ge(s["v_step"], v_at.after("sgw_used", n + 1))
                        v.tensor_scalar(run, run, half, None, ALU.subtract).then_inc(s["pre"], 1)
            def prep(q):
                w = q % 2
                v.wait_ge(s["kdb"], q + 1)
                v.wait_ge(s["ex"], q + 1)
                v.wait_ge(s["kk_mm"], q + 1)
                if q == 0:
                    v.wait_ge(s["pool_zero"], 3)
                else:
                    v.wait_ge(s["m_mm"], 8 * q)
                    v.wait_ge(s["bt_mm"], q)
                kk_q = kkT[:, q, :].rearrange("p (g t) -> p g t", g=G)
                r_q = rT[:, q, :].rearrange("p (g t) -> p g t", g=G)
                for d in range(2):
                    up, at_r, at_a = (0, 1, 0) if d == 0 else (1, 0, 1)
                    down, at_k = (1, 1) if d == 0 else (0, 0)
                    v.tensor_tensor(ra[:, w, :, d, 0, :], r_q, Ex[:, up, d, :, at_r:at_r + T], ALU.mult)
                    v.scalar_tensor_tensor(ra[:, w, :, d, 1, :], kk_q, -1.0, Ex[:, up, d, :, at_a:at_a + T], ALU.mult, ALU.mult)
                    for k, src in enumerate((kd, bv)):
                        for h in range(2):
                            half = slice(HD * h, HD * h + HD)
                            last = v.tensor_tensor(kbp[half, :, k, h, d, :], src[half, d, :].rearrange("p (g t) -> p g t", g=G),
                                                   Ex[half, down, d, :, at_k:at_k + T], ALU.mult)
                last.then_inc(s["prep"], 1)

            order, tapped = tap_order(), [0]

            def conv_taps(count):
                for n in range(tapped[0], min(tapped[0] + count, len(order))):
                    c, tap, former = order[n]
                    wcol = chan[:, c, tap:tap + 1]
                    if tap == 0:
                        v.wait_ge(s["kk"], taken("cv", c))
                        v.tensor_scalar(acc[:, c, :], u[:, c, 0:A_COLS], wcol, chan[:, c, C_CONVB:C_CONVB + 1],
                                        ALU.mult, ALU.add).then_inc(s["conv"], 1)
                    else:
                        v.wait_ge(s["conv"], former)
                        v.scalar_tensor_tensor(acc[:, c, :], u[:, c, tap:tap + A_COLS], wcol, acc[:, c, :],
                                               ALU.mult, ALU.add).then_inc(s["conv"], 1)
                tapped[0] += count

            def unit_kk(q):
                v.reciprocal(rn[:, q, :], rn[:, q, :]).then_inc(s["v_step"], v_at.mark("kk_rec"))
                v.wait_ge(s["v_step"], v_at.after("kk_rec", q + 1))
                v.tensor_tensor(kkT[:, q, :], kkT[:, q, :], rn[:, q, :], ALU.mult).then_inc(s["kk_mm"], 1)

            def take_k(q):
                v.wait_ge(s["a_sig"], taken("k", q))
                v.tensor_scalar(kkT[:, q, :], kT[:, q, :], chan[:, q, C_KK:C_KK + 1], None, ALU.mult).then_inc(s["kk_raw"], 1)

            for n, (kind, q, d, e) in enumerate(items):
                if kind == "k":
                    conv_taps(TAPS_K)
                    take_k(q)
                if e != "v":
                    continue
                if kind == "r":
                    conv_taps(TAPS_R)
                out = bank_of(n)
                v.wait_ge(s["kv_mm"], n - 18)
                if kind == "r":
                    v.tensor_copy(rT[:, q, :], out[:, 0:N]).then_inc(s["kk"], 1)
                elif kind == "kn":
                    v.tensor_scalar(rn[:, q, :], out[:, 0:N], 1e-24, None, ALU.max).then_inc(s["kk"], 1)
                    if q == Q - 1:
                        v.wait_ge(s["kk_sqrt"], 1)
                        for c in range(Q - 1):
                            unit_kk(c)
                elif kind == "v":
                    if q == 0:
                        prep(0)
                    v.tensor_copy(V[:, q, :], out).then_inc(s["kk"], 1)
                    if q == G - 1:
                        unit_kk(Q - 1)
                elif kind == "cv":
                    v.wait_ge(s["a_sig"], emptied(n + 1, "a"))
                    v.wait_ge(s["pool_zero"], 2)
                    v.tensor_tensor(u[:, q, U_CTX:U_CTX + T], out[:, 0:T], sgc[:, q, 0:T], ALU.mult)
                    v.tensor_tensor(u[:, q, U_LAT:U_LAT + 2 * U_STEP].rearrange("p (r c) -> p r c", r=2)[:, :, 0:SEG],
                                    out[:, T:N].rearrange("p (r c) -> p r c", r=2),
                                    sgc[:, q, T:N].rearrange("p (r c) -> p r c", r=2), ALU.mult).then_inc(s["kk"], 1)
                    if q < 3:
                        conv_taps(TAPS_U[q])

            def norm_centre(r):
                v.wait_ge(s["gn_mm"], r + 1)
                v.scalar_tensor_tensor(oc[:, r, :], ps[5][:, 0:N], -1.0 / HD, oT[:, r, :], ALU.mult, ALU.add)\
                    .then_inc(s["gn_cen"], 1)

            def norm_bonus(r):
                v.wait_ge(s["gn_std"], r + 1)
                v.wait_ge(s["vt"], r + 1)
                v.tensor_tensor(rkk[:, r, :], ps[7][:, N:2 * N], vT[:, r, :], ALU.mult).then_inc(s["bo"], 1)

            def norm_rest(r):
                v.wait_ge(s["bo"], r + 1)
                v.reciprocal(sq[:, r, :], sq[:, r, :]).then_inc(s["v_step"], v_at.mark("gn_rec"))
                v.wait_ge(s["v_step"], v_at.after("gn_rec", r + 1))
                v.tensor_tensor(oc[:, r, :], oc[:, r, :], sq[:, r, :], ALU.mult).then_inc(s["v_step"], v_at.mark("gn_1"))
                v.wait_ge(s["v_step"], v_at.after("gn_1", r + 1))
                v.tensor_scalar(oc[:, r, :], oc[:, r, :], chan[:, r, C_GNG:C_GNG + 1], chan[:, r, C_GNB:C_GNB + 1],
                                ALU.mult, ALU.add).then_inc(s["v_step"], v_at.mark("gn_2"))
                v.wait_ge(s["v_step"], v_at.after("gn_2", r + 1))
                v.tensor_tensor(oc[:, r, :], oc[:, r, :], rkk[:, r, :], ALU.add).then_inc(s["v_step"], v_at.mark("gn_3"))
                v.wait_ge(s["v_step"], v_at.after("gn_3", r + 1))
                v.tensor_tensor(oT[:, r, :], oc[:, r, :], gT[:, r, :], ALU.mult).then_inc(s["gn_out"], 1)

            def level_mask(lv):
                return level[:, lv, :, :].unsqueeze(2).broadcast_to([P, 2, 2, T])

            def twice(ap):
                return ap.unsqueeze(1).broadcast_to([P, 2, 2, T])

            for q in range(Q):
                for g in range(G):
                    for i in range(4):
                        h, d = divmod(i, 2)
                        n = 8 * q + 4 * g + i
                        v.wait_ge(s["m_mm"], n + 1)
                        v.tensor_tensor(LT[:, g, h, d].rearrange("p (k a) t -> p k a t", k=2),
                                        ps[6 + n % 2].rearrange("p (k a t) -> p k a t", k=2, a=2),
                                        mask_lt[:, d].unsqueeze(1).broadcast_to([P, 2, 2, T]), ALU.mult)\
                            .then_inc(s["m_ev"], 1)
                    v.wait_ge(s["m_ev"], 8 * q + 4 * g + 4)
                    v.tensor_tensor(LT[:, g, :, 0, 3, :], LT[:, g, :, 0, 3, :], LT[:, g, :, 1, 3, :], ALU.add).then_inc(s["lsum"], 1)
                v.wait_ge(s["level"], 1)
                if q < Q - 1:
                    conv_taps(TAPS_BEFORE)
                if q > 0:
                    norm_centre(q - 1)
                for lv in range(LEVELS):
                    if q < Q - 1:
                        conv_taps(TAPS_BESIDE[q])
                    for g in range(G):
                        parts = 22 * q + (4 * (lv - 1) + 2 * g + 1 if lv < LEVELS - 1 else 20 + g)
                        if lv == 0:
                            v.wait_ge(s["xy"], 2 * q + g + 1)
                            v.wait_ge(s["lsum"], 2 * q + g + 1)
                        if lv < LEVELS - 1:
                            v.wait_ge(s["d_mm"], 12 * q + 2 * lv + g + 1)
                            if lv > 0:
                                v.wait_ge(s["part_up"], parts)
                            v.copy_predicated(X[:, g], level_mask(lv), twice(
                                ps[2 + 2 * g][:, 0:2 * P].rearrange("p (h t) -> p h t", h=2))).then_inc(s["x_up"], 1)
                        if lv == 0:
                            v.copy_predicated(Y[:, g, 0:3:2], level_mask(lv), twice(LT[:, g, :, 0, 3, :])).then_inc(s["y_up"], 1)
                        else:
                            v.wait_ge(s["e_mm"], 12 * q + 2 * (lv - 1) + g + 1)
                            v.wait_ge(s["part_up"], parts + 1)
                            to = X[:, g] if lv == LEVELS - 1 else Y[:, g, 0:2] if lv % 2 else Y[:, g, 0:3:2]
                            v.copy_predicated(to, level_mask(lv), twice(
                                ps[3 + 2 * g][:, 0:2 * P].rearrange("p (h t) -> p h t", h=2))).then_inc(s["y_up"], 1)
                    if lv == 2 and q > 0:
                        norm_bonus(q - 1)
                    if q == Q - 1 and lv == 2:
                        v.wait_ge(s["cm_mm"], 1)
                        for c in range(Q):
                            v.scalar_tensor_tensor(acc[:, c, :], ps[6][:, 0:A_COLS], -1.0 / CH, acc[:, c, :],
                                                   ALU.mult, ALU.add).then_inc(s["c_cen"], 1)
                    if q == Q - 1 and lv == 4:
                        v.wait_ge(s["c_std"], 1)
                        v.reciprocal(crs, crs).then_inc(s["v_step"], v_at.mark("c_rec"))
                        v.wait_ge(s["v_step"], v_at.after("c_rec", 1))
                        for c in range(Q):
                            v.tensor_tensor(acc[:, c, :], acc[:, c, :], crs, ALU.mult).then_inc(s["v_step"], v_at.mark("c_n1"))
                        for c in range(Q):
                            v.wait_ge(s["v_step"], v_at.after("c_n1", c + 1))
                            v.tensor_scalar(acc[:, c, :], acc[:, c, :], chan[:, c, C_LNG:C_LNG + 1],
                                            chan[:, c, C_LNB:C_LNB + 1], ALU.mult, ALU.add).then_inc(s["c_n2"], 1)
                if q > 0:
                    norm_rest(q - 1)
                if q < Q - 1:
                    prep(q + 1)
                v.wait_ge(s["ada_acc"], 4 * (q + 1))
                b = q // 2
                if q == 0:
                    v.wait_ge(s["in_mod"], 80)
                v.tensor_tensor(mod[:, b, :], ps[3], madd[:, b, :] if q % 2 == 0 else mod[:, b, :], ALU.add)\
                    .then_inc(s["mod_t"], 1)
                if q % 2:
                    v.wait_ge(s["mod_t"], q + 1)
                    v.scalar_tensor_tensor(mod[:, b, :], mod[:, b, :], const[:, K_ONE + 1 + b:K_ONE + 2 + b], mmul[:, b, :],
                                           ALU.add, ALU.mult).then_inc(s["mod"], 1)
            norm_centre(Q - 1)
            v.wait_ge(s["c_sig"], 1)
            for q in range(Q):
                v.tensor_tensor(cvT[:, q, 0:T], acc[:, q, 0:T], csg[:, q, 0:T], ALU.mult)
                for r in range(2):
                    c0 = A_LAT + r * U_STEP
                    last = v.tensor_tensor(cvT[:, q, T + SEG * r:T + SEG * r + SEG], acc[:, q, c0:c0 + SEG],
                                           csg[:, q, c0:c0 + SEG], ALU.mult)
                last.then_inc(s["c_out"], 1)
            norm_bonus(Q - 1)
            norm_rest(Q - 1)
            v.wait_ge(s["gtb_ev"], 4)
            v.wait_ge(s["in_x1"], 16)
            for g in range(G):
                v.wait_ge(s["mix_ss"], 2 * g + 2)
                v.tensor_tensor(rsm[:, g:g + 1], ssm[:, 2 * g:2 * g + 1], ssm[:, 2 * g + 1:2 * g + 2], ALU.add)\
                    .then_inc(s["mix_rs"], 1)
                v.wait_ge(s["mix_rec"], g + 1)
                v.reciprocal(rsm[:, g:g + 1], rsm[:, g:g + 1]).then_inc(s["v_step"], v_at.mark("mix_rec"))
                v.wait_ge(s["v_step"], v_at.after("mix_rec", g + 1))
                for n in (2 * g, 2 * g + 1):
                    cols = slice(n % 2 * 512, n % 2 * 512 + 512)
                    v.scalar_tensor_tensor(mixn[:, g, cols], ps[n], rsm[:, g:g + 1], gtb[:, n, :], ALU.mult, ALU.mult)\
                        .then_inc(s["mul1"], 1)
                for n in (2 * g, 2 * g + 1):
                    cols = slice(n % 2 * 512, n % 2 * 512 + 512)
                    v.wait_ge(s["mul1"], n + 1)
                    v.tensor_tensor(x1[:, g, cols], x1[:, g, cols], mixn[:, g, cols], ALU.add).then_inc(s["x1"], 1)
            v.wait_ge(s["a2b"], 1)
            for g in range(G):
                v.wait_ge(s["rs_2"], g + 1)
                v.reciprocal(rs2[:, g:g + 1], rs2[:, g:g + 1]).then_inc(s["v_step"], v_at.mark("rec_2"))
                v.wait_ge(s["v_step"], v_at.after("rec_2", g + 1))
                for n in (2 * g, 2 * g + 1):
                    cols = slice(n % 2 * 512, n % 2 * 512 + 512)
                    v.scalar_tensor_tensor(h2[:, g, cols], x1[:, g, cols], rs2[:, g:g + 1], ps[4 + n], ALU.mult, ALU.mult)\
                        .then_inc(s["v_step"], v_at.mark("h2_1"))
                v.wait_ge(s["b2b"], g + 1)
                for n in (2 * g, 2 * g + 1):
                    cols = slice(n % 2 * 512, n % 2 * 512 + 512)
                    v.wait_ge(s["v_step"], v_at.after("h2_1", n + 1))
                    v.tensor_tensor(h2[:, g, cols], h2[:, g, cols], ps[n], ALU.add).then_inc(s["h2"], 1)
            v.memset(ext[:, :, E:40], -BIG)
            v.memset(rank[:, :, E:E + 2], -1.0)
            v.memset(b8[:, :, :], -BIG).then_inc(s["v_step"], v_at.mark("ext0"))
            v.wait_ge(s["in_router"], 64)
            for g in range(G):
                v.wait_ge(s["logits"], g + 1)
                v.tensor_tensor(ext[:, g, 0:E], ps[g][:, 0:E], rb, ALU.add).then_inc(s["v_step"], v_at.mark("lg"))
            v.wait_ge(s["v_step"], v_at.after("ext0", 1))
            for g in range(G):
                v.wait_ge(s["v_step"], v_at.after("lg", g + 1))
                v.max(m8[:, g, :], ext[:, g, 0:E]).then_inc(s["v_step"], v_at.mark("t8"))
            for g in range(G):
                v.wait_ge(s["v_step"], v_at.after("t8", g + 1))
                v.tensor_copy(b8[:, g, 0:TOPK], m8[:, g, 0:TOPK]).then_inc(s["v_step"], v_at.mark("b8"))
                v.tensor_scalar(negm[:, g:g + 1], m8[:, g, 0:1], -1.0, None, ALU.mult).then_inc(s["negm"], 1)
                v.wait_ge(s["v_step"], v_at.after("b8", g + 1))
                v.match_replace(rep[:, g, :], b8[:, g, :], ext[:, g, :], BIG).then_inc(s["v_step"], v_at.mark("rep"))
            for g in range(G):
                v.wait_ge(s["v_step"], v_at.after("rep", g + 1))
                v.tensor_tensor(sel_m[:, g, :], rep[:, g, 0:E], ext[:, g, 0:E], ALU.not_equal).then_inc(s["selm"], 1)
            v.wait_ge(s["rk_mm"], 1)
            for g in range(G):
                v.scalar_tensor_tensor(rank[:, g, 0:E], ps[2][:, g * E:(g + 1) * E], 1.0, sel_m[:, g, :], ALU.add, ALU.mult)\
                    .then_inc(s["v_step"], v_at.mark("rank1"))
            for g in range(G):
                v.wait_ge(s["v_step"], v_at.after("rank1", g + 1))
                v.tensor_scalar(rank[:, g, 0:E], rank[:, g, 0:E], -1.0, None, ALU.add).then_inc(s["rank2"], 1)
            v.wait_ge(s["rank2"], 2)
            choose(v, 0)
            choose_bias(v, 0)
            v.reduce_max(most, ps[2][:, 2 * E:3 * E], AX.X).then_inc(s["v_step"], v_at.mark("cnt"))
            v.wait_ge(s["v_step"], v_at.after("cnt", 1))
            v.tensor_copy(most_i, most).then_inc(s["flag"], 1)
            for g in range(G):
                v.wait_ge(s["selm"], g + 1)
                v.wait_ge(s["expm"], g + 1)
                v.tensor_tensor(ex[:, g, :], ex[:, g, :], sel_m[:, g, :], ALU.mult).then_inc(s["v_step"], v_at.mark("exm"))
                v.wait_ge(s["v_step"], v_at.after("exm", g + 1))
                v.reduce_sum(gsum[:, g:g + 1], ex[:, g, :], AX.X).then_inc(s["v_step"], v_at.mark("gsum"))
                v.wait_ge(s["v_step"], v_at.after("gsum", g + 1))
                v.reciprocal(grec[:, g:g + 1], gsum[:, g:g + 1]).then_inc(s["v_step"], v_at.mark("grec"))
                v.wait_ge(s["v_step"], v_at.after("grec", g + 1))
                v.tensor_scalar(gate[:, g, 0:E], ex[:, g, :], grec[:, g:g + 1], None, ALU.mult).then_inc(s["gate"], 1)
            v.memset(yacc, 0.0).then_inc(s["cleared"], 1)
            v.memset(outp, 0.0).then_inc(s["outp_ready"], 4)
            v.memset(GT, 0.0).then_inc(s["gt_ready"], 1)
            v.wait_ge(s["cleared"], 1)
            v.wait_ge(s["gate"], 2)
            with v.Fori(0, E // 2) as i:
                dve_pair(v, 0, 0, i)
            v.wait_ge(s["flag"], 1)
            more = v.value_load(most_i[0:1, 0:1], min_val=0, max_val=N)
            with v.If(more > S):
                with v.Fori(1, N // S) as turn:
                    v.tensor_scalar(rank.rearrange("p g e -> p (g e)"), rank.rearrange("p g e -> p (g e)"),
                                    -float(S), None, ALU.add).then_inc(s["shifted"], 1)
                    v.wait_ge(s["shifted"], turn)
                    v.wait_ge(s["gathered"], turn * (E + 2))
                    choose(v, 0)
                    choose_bias(v, 0)
                    with v.Fori(0, E // 2) as i:
                        dve_pair(v, turn * (E // 2), turn, i)
                add_outputs(v, (N // S) * (E // 2) + 1, "y_sum")
            with v.Else():
                add_outputs(v, E // 2 + 1, "y_sum")
            for n in range(4):
                g, cols = n // 2, slice(n % 2 * 512, n % 2 * 512 + 512)
                v.wait_ge(s["gt2b"], g + 1)
                v.wait_ge(s["y_sum"], n + 1)
                v.tensor_tensor(scaled[:, g, cols], yacc[:, g, cols], ps[n], ALU.mult)\
                    .then_inc(s["v_step"], v_at.mark("fin1"))
            for g in range(G):
                v.wait_ge(s["y_rs"], g + 1)
                v.reciprocal(rsm[:, g:g + 1], rsm[:, g:g + 1]).then_inc(s["v_step"], v_at.mark("y_rec"))
                v.wait_ge(s["v_step"], v_at.after("y_rec", g + 1))
                for n in (2 * g, 2 * g + 1):
                    cols = slice(n % 2 * 512, n % 2 * 512 + 512)
                    v.scalar_tensor_tensor(x1[:, g, cols], scaled[:, g, cols], rsm[:, g:g + 1], x1[:, g, cols],
                                           ALU.mult, ALU.add).then_inc(s["fin"], 1)


def constants():
    c = np.zeros((P, K_N), np.float32)
    i = np.arange(P)
    c[:, K_ID:K_ID + P] = np.eye(P)
    c[:, K_HEAD:K_HEAD + P] = (i[:, None] // HD) == (i[None, :] // HD)
    c[:, K_ONES:K_ONES + P] = 1.0
    c[:, K_UPPER:K_UPPER + P] = i[:, None] < i[None, :]
    m = np.stack([np.stack([i[:, None] <= i[None, :], i[:, None] < i[None, :]], 1),
                  np.stack([i[:, None] >= i[None, :], i[:, None] > i[None, :]], 1)], 1)
    c[:, K_MASK:K_MASK + 512] = m.reshape(P, 512)
    c[:, K_IOTA:K_IOTA + S] = np.arange(S)
    c[:, K_EPS:K_EPS + 3] = (1e-6, 1e-5, 64e-5)
    for cc in (2, 3, 8, 9):
        b, j = divmod(cc, 4)
        c[32 * j:32 * j + G, K_ONE + b] = 1.0
    lv = np.zeros((P, LEVELS, 2, T), np.float32)
    part = np.zeros((P, LEVELS - 2, T), np.float32)
    lower = i[:, None] >= i[None, :]
    for n in range(LEVELS):
        b = 1 << n
        low = (i[:, None] // b % 2 == 1) & (i[:, None] // b == i[None, :] // b + 1)
        even = (i[:, None] // (2 * b) % 2 == 0)
        if n < LEVELS - 1:
            lv[:, n, 0], lv[:, n, 1] = low | low.T, np.where(even, low, low.T)
        else:
            lv[:, n, 0], lv[:, n, 1] = low.T, low
        if 1 <= n < LEVELS - 1:
            part[:, n - 1] = np.where(even, lower, lower.T)
    return c, lv, part


def kernel(**inputs):
    import concourse.bacc as _bacc
    from concourse.bass_utils import run_bass_kernel_spmd as _run

    inp = {k: np.asarray(v) for k, v in inputs.items()}
    L = {k: inp[k][0] for k in inp if k not in ("x_prompt", "x_sample", "c", "c_ctx", "state_wkv_fwd", "state_wkv_bwd")}
    const, lv, part = constants()

    def chan_cols(v):
        return v.reshape(-1, Q, P).transpose(2, 1, 0)

    mod = np.zeros((2, P, 3 * 512), np.float32)
    rows = {0: L["ada_b"].reshape(12, 512)}
    gains = np.ones((12, 512), np.float32)
    for at, name in ((2, "pre_mix_g"), (4, "post_mix_g"), (8, "pre_ffn_g"), (10, "post_ffn_g")):
        gains[at:at + 2] = L[name].reshape(2, 512)
    rows[1] = gains
    for n in range(2):
        for cc in range(12):
            b, j = divmod(cc, 4)
            mod[n, 32 * j:32 * j + G, b * 512:(b + 1) * 512] = rows[n][cc]
    arrays = {
        "x": np.concatenate([inp["x_prompt"][0], inp["x_sample"][0]]),
        "cond": np.stack([inp["c_ctx"], inp["c"][0]]).reshape(G, KC, P).transpose(2, 1, 0),
        "ada_w": L["ada_w"], "mod": mod, "w_in": L["w_in"], "w_out": L["w_out"],
        "chan": np.concatenate([chan_cols(L[n].reshape(-1, CH)) for n in (
            "conv_w", "conv_b", "conv_ln_g", "conv_ln_b", "rw_w0", "rw_a0", "rw_k_k", "rw_k_a", "rw_r_k",
            "rw_gn_g", "rw_gn_b")], axis=2),
        "lora1": np.concatenate([L["rw_w1"][0], L["rw_w1"][1], L["rw_a1"][0], L["rw_a1"][1], L["rw_g1"]], axis=1)
        .reshape(KC, P, 3 * P).transpose(1, 0, 2),
        "w2": L["rw_w2"], "a2": L["rw_a2"], "g2": L["rw_g2"],
        "s0": np.stack([inp["state_wkv_fwd"][0, 0], inp["state_wkv_bwd"][0, 0]]).transpose(0, 1, 3, 2),
        "router_w": L["router_w"], "router_b": L["router_b"],
        "w_gu": L["w_gu"], "b_gu": L["b_gu"], "w_down": L["w_down"], "b_down": L["b_down"],
        "const": const, "level": lv, "part": part,
    }
    nc = _bacc.Bacc("TRN2", target_bir_lowering=False, num_devices=1)
    args, feed = [], {}
    for name, a in arrays.items():
        a = np.ascontiguousarray(a)
        feed[f"in_{name}"] = a
        args.append(nc.dram_tensor(f"in_{name}", a.shape, mybir.dt.from_np(a.dtype), kind="ExternalInput").ap())
    outs = [("y_prompt", (T, D)), ("y_sample", (T, D)), ("st_f", (8, HD, HD)), ("st_b", (8, HD, HD))]
    for name, shape in outs:
        args.append(nc.dram_tensor(name, shape, FP32, kind="ExternalOutput").ap())
    build(nc, *args)
    r = _run(nc, [feed], core_ids=[0]).results[0]
    return (r["y_prompt"].reshape(1, T, D), r["y_sample"].reshape(1, T, D),
            r["st_f"].reshape(1, 1, 8, HD, HD), r["st_b"].reshape(1, 1, 8, HD, HD))
```
